# Optimizing a Trainium2 kernel written in Bass

```python
import math
import jax, jax.numpy as jnp
from jax import lax
import numpy as np

D_MODEL = 2048
BATCH = 1
SEQ = 256
DEPTH = 2

GRID_W = 64
CTX_LEN = 256
EPS = 1e-6
NEG = -1e30

HEAD_DIM = 128
W_A = D_MODEL // 4
W_B = D_MODEL // 2
W_C = D_MODEL // 4
MIX_W = W_A + W_B + W_C

CHUNK = 128
A_GROUPS = W_A // HEAD_DIM

B_HEADS = W_B // HEAD_DIM
Q_LORA = D_MODEL // 4
KV_LORA = 512
NOPE_DIM = 128
ROPE_DIM = 64
V_DIM = 128
MLA_SCALE = (NOPE_DIM + ROPE_DIM) ** -0.5
ROPE_THETA = 10000.0

C_HEADS = W_C // HEAD_DIM
MAX_KH = 8
KW = 16
C_SCALE = HEAD_DIM ** -0.5

Q_BLOCK = 128
SPLIT_WIDTHS = (W_A, W_A, W_A, Q_LORA, KV_LORA, ROPE_DIM, W_B, W_C, W_C, W_C, W_C)
IN_W = 3 * W_A + Q_LORA + KV_LORA + ROPE_DIM + W_B + 4 * W_C

kernel_name = "hybrid_gmlp_mla_natten_prefix_block"

def rmsnorm(x, g):
    xf = x.astype(jnp.float32)
    y = xf * lax.rsqrt(jnp.mean(xf * xf, axis=-1, keepdims=True) + EPS)
    return (y * g.astype(jnp.float32)).astype(x.dtype)

def split_in(z):
    offs, acc = [], 0
    for w in SPLIT_WIDTHS[:-1]:
        acc += w
        offs.append(acc)
    return jnp.split(z, offs, axis=-1)

def axial_angles(n_tokens):
    t = jnp.arange(n_tokens)
    row = (t // GRID_W).astype(jnp.float32)
    col = (t % GRID_W).astype(jnp.float32)
    n_freq = ROPE_DIM // 4
    inv = ROPE_THETA ** (-jnp.arange(n_freq, dtype=jnp.float32) / n_freq)
    return row[:, None] * inv, col[:, None] * inv

def _rotate(x, ang):
    m = x.shape[-1] // 2
    x1, x2 = x[..., :m], x[..., m:]
    cos = jnp.cos(ang).astype(x.dtype)
    sin = jnp.sin(ang).astype(x.dtype)
    return jnp.concatenate([x1 * cos - x2 * sin, x2 * cos + x1 * sin], axis=-1)

def axial_rope(x, ang_row, ang_col):
    half = ROPE_DIM // 2
    return jnp.concatenate([_rotate(x[..., :half], ang_row), _rotate(x[..., half:], ang_col)], axis=-1)

def chunk_gmlp(u, v, sgu_g, w_s, b_s):
    B, N, _ = u.shape
    u = jax.nn.gelu(u)
    v = rmsnorm(jax.nn.gelu(v), sgu_g).reshape(B, N // CHUNK, CHUNK, A_GROUPS, HEAD_DIM)
    s = jnp.einsum('gpq,bnqgc->bnpgc', w_s, v) + b_s.T[None, None, :, :, None]
    return u * s.reshape(B, N, W_A)

def mla_q(cq, qa_g, w_uq):
    B, N, _ = cq.shape
    q = (rmsnorm(cq, qa_g) @ w_uq).reshape(B, N, B_HEADS, NOPE_DIM + ROPE_DIM)
    return q[..., :NOPE_DIM], q[..., NOPE_DIM:]

def mla_kv(ckv, kva_g, w_ukv):
    B, N, _ = ckv.shape
    kv = (rmsnorm(ckv, kva_g) @ w_ukv).reshape(B, N, B_HEADS, NOPE_DIM + V_DIM)
    return kv[..., :NOPE_DIM], kv[..., NOPE_DIM:]

def mla_latent_attention(qn, qr, kn, kr, v, kn_c, kr_c, v_c):
    B, S, H, _ = qn.shape
    n_blocks = S // Q_BLOCK

    def block(i):
        qbn = lax.dynamic_slice_in_dim(qn, i * Q_BLOCK, Q_BLOCK, axis=1)
        qbr = lax.dynamic_slice_in_dim(qr, i * Q_BLOCK, Q_BLOCK, axis=1)
        s_lat = jnp.einsum('bqhd,bkhd->bhqk', qbn, kn) + jnp.einsum('bqhr,bkr->bhqk', qbr, kr)
        s_ctx = jnp.einsum('bqhd,bkhd->bhqk', qbn, kn_c) + jnp.einsum('bqhr,bkr->bhqk', qbr, kr_c)
        s = jnp.concatenate([s_lat, s_ctx], axis=-1).astype(jnp.float32) * MLA_SCALE
        p = jax.nn.softmax(s, axis=-1).astype(v.dtype)
        return (jnp.einsum('bhqk,bkhd->bqhd', p[..., :S], v)
                + jnp.einsum('bhqk,bkhd->bqhd', p[..., S:], v_c))

    out = lax.map(block, jnp.arange(n_blocks))
    return out.transpose(1, 0, 2, 3, 4).reshape(B, S, H * V_DIM)

def mla_context_attention(qn, qr, kn, kr, v):
    B, L, H, _ = qn.shape
    s = jnp.einsum('bqhd,bkhd->bhqk', qn, kn) + jnp.einsum('bqhr,bkr->bhqk', qr, kr)
    p = jax.nn.softmax(s.astype(jnp.float32) * MLA_SCALE, axis=-1).astype(v.dtype)
    return jnp.einsum('bhqk,bkhd->bqhd', p, v).reshape(B, L, H * V_DIM)

def dense_attention(q, k, v, scale):
    B, L, H, D = q.shape
    s = jnp.einsum('bqhd,bkhd->bhqk', q, k).astype(jnp.float32) * scale
    p = jax.nn.softmax(s, axis=-1).astype(v.dtype)
    return jnp.einsum('bhqk,bkhd->bqhd', p, v).reshape(B, L, H * D)

def natten_latent(q, k, v, k_c, v_c, rpb):
    B, S, H, D = q.shape
    rows = S // GRID_W
    kh = min(MAX_KH, rows)
    r = jnp.arange(rows)
    col = jnp.arange(GRID_W)
    r0 = jnp.clip(r - kh // 2, 0, rows - kh)
    row_idx = r0[:, None] + jnp.arange(kh)[None, :]
    c0 = jnp.clip(col - KW // 2, 0, GRID_W - KW)
    col_ok = (col[None, :] >= c0[:, None]) & (col[None, :] < c0[:, None] + KW)
    dr = row_idx - r[:, None] + (MAX_KH - 1)
    dc = jnp.clip(col[None, :] - col[:, None], -(KW - 1), KW - 1) + (KW - 1)
    bias = rpb[:, dr[:, None, :, None], dc[None, :, None, :]].astype(jnp.float32)
    bias = jnp.where(col_ok[None, None, :, None, :], bias, NEG)
    bias = bias.reshape(H, rows, GRID_W, kh * GRID_W).transpose(1, 0, 2, 3)

    qg = q.reshape(B, rows, GRID_W, H, D)
    kg = k.reshape(B, rows, GRID_W, H, D)
    vg = v.reshape(B, rows, GRID_W, H, D)
    n_keys = kh * GRID_W
    ks = kg[:, row_idx].reshape(B, rows, n_keys, H, D)
    vs = vg[:, row_idx].reshape(B, rows, n_keys, H, D)
    s_nb = jnp.einsum('brqhd,brkhd->brhqk', qg, ks).astype(jnp.float32) * C_SCALE + bias[None]
    s_cx = jnp.einsum('brqhd,blhd->brhql', qg, k_c).astype(jnp.float32) * C_SCALE
    p = jax.nn.softmax(jnp.concatenate([s_nb, s_cx], axis=-1), axis=-1).astype(v.dtype)
    o = (jnp.einsum('brhqk,brkhd->brqhd', p[..., :n_keys], vs)
         + jnp.einsum('brhql,blhd->brqhd', p[..., n_keys:], v_c))
    return o.reshape(B, S, H * D)

def hybrid_layer(x, xc, mod, mod_c, norm_g, w_in, qa_g, kva_g, w_uq, w_ukv,
                 sgu_g, w_s, b_s, rpb, w_out, ang_r, ang_c, ctx_out):
    B, S, _ = x.shape
    L = xc.shape[1]
    shift, scale, gate = jnp.split(mod, 3, axis=-1)
    shift_c, scale_c, gate_c = jnp.split(mod_c, 3, axis=-1)
    h = rmsnorm(x, norm_g) * (1.0 + scale[:, None, :]) + shift[:, None, :]
    hc = rmsnorm(xc, norm_g) * (1.0 + scale_c) + shift_c

    u, v_a, g_a, cq, ckv, kr, g_b, q_c, k_c, v_c, g_c = split_in(h @ w_in)
    (u_x, v_ax, g_ax, cq_x, ckv_x, kr_x, g_bx,
     q_cx, k_cx, v_cx, g_cx) = split_in(hc @ w_in)

    a_out = chunk_gmlp(u, v_a, sgu_g, w_s, b_s)

    qn, qr = mla_q(cq, qa_g, w_uq)
    qr = axial_rope(qr, ang_r[:, None, :], ang_c[:, None, :])
    kn, v_b = mla_kv(ckv, kva_g, w_ukv)
    kr = axial_rope(kr, ang_r, ang_c)
    kn_x, v_bx = mla_kv(ckv_x, kva_g, w_ukv)
    b_out = mla_latent_attention(qn, qr, kn, kr, v_b, kn_x, kr_x, v_bx)

    hd = lambda t, n: t.reshape(B, n, C_HEADS, HEAD_DIM)
    k_cx_h, v_cx_h = hd(k_cx, L), hd(v_cx, L)
    c_out = natten_latent(hd(q_c, S), hd(k_c, S), hd(v_c, S), k_cx_h, v_cx_h, rpb)

    y = jnp.concatenate([a_out * jax.nn.silu(g_a), b_out * jax.nn.silu(g_b),
                         c_out * jax.nn.silu(g_c)], axis=-1) @ w_out
    x_new = x + gate[:, None, :] * y

    if ctx_out:
        a_x = chunk_gmlp(u_x, v_ax, sgu_g, w_s, b_s)
        qn_x, qr_x = mla_q(cq_x, qa_g, w_uq)
        b_x = mla_context_attention(qn_x, qr_x, kn_x, kr_x, v_bx)
        c_x = dense_attention(hd(q_cx, L), k_cx_h, v_cx_h, C_SCALE)
        yc = jnp.concatenate([a_x * jax.nn.silu(g_ax), b_x * jax.nn.silu(g_bx),
                              c_x * jax.nn.silu(g_cx)], axis=-1) @ w_out
        xc = xc + gate_c * yc
    return x_new, xc

def setup_inputs(seed: int = 0) -> dict:
    key = jax.random.key(seed)
    ks = jax.random.split(key, 20)
    nrm = lambda k, shape, s: jax.random.normal(k, shape, jnp.float32) * s
    return {
        "x": nrm(ks[0], (BATCH, SEQ, D_MODEL), 1.0),
        "c": nrm(ks[1], (BATCH, D_MODEL), 1.0),
        "ctx": nrm(ks[2], (BATCH, CTX_LEN, D_MODEL), 1.0),
        "c_ctx": nrm(ks[3], (D_MODEL,), 1.0),
        "w_ada": nrm(ks[4], (DEPTH, D_MODEL, 3 * D_MODEL), 0.5 * D_MODEL ** -0.5),
        "b_ada": nrm(ks[5], (DEPTH, 3 * D_MODEL), 0.02),
        "norm_g": 1.0 + nrm(ks[6], (DEPTH, D_MODEL), 0.02),
        "w_in": nrm(ks[7], (DEPTH, D_MODEL, IN_W), D_MODEL ** -0.5),
        "qa_g": 1.0 + nrm(ks[8], (DEPTH, Q_LORA), 0.02),
        "kva_g": 1.0 + nrm(ks[9], (DEPTH, KV_LORA), 0.02),
        "w_uq": nrm(ks[10], (DEPTH, Q_LORA, B_HEADS * (NOPE_DIM + ROPE_DIM)), Q_LORA ** -0.5),
        "w_ukv": nrm(ks[11], (DEPTH, KV_LORA, B_HEADS * (NOPE_DIM + V_DIM)), KV_LORA ** -0.5),
        "sgu_g": 1.0 + nrm(ks[12], (DEPTH, W_A), 0.02),
        "w_s": nrm(ks[13], (DEPTH, A_GROUPS, CHUNK, CHUNK), CHUNK ** -0.5),
        "b_s": 1.0 + nrm(ks[14], (DEPTH, A_GROUPS, CHUNK), 0.02),
        "rpb": nrm(ks[15], (DEPTH, C_HEADS, 2 * MAX_KH - 1, 2 * KW - 1), 0.1),
        "w_out": nrm(ks[16], (DEPTH, MIX_W, D_MODEL), MIX_W ** -0.5),
        "final_g": 1.0 + nrm(ks[17], (D_MODEL,), 0.02),
    }

def reference(x, c, ctx, c_ctx, w_ada, b_ada, norm_g, w_in, qa_g, kva_g, w_uq, w_ukv,
              sgu_g, w_s, b_s, rpb, w_out, final_g):
    silu_c = jax.nn.silu(c)
    silu_cc = jax.nn.silu(c_ctx)
    ang_r, ang_c = axial_angles(x.shape[1])
    xc = ctx
    for l in range(DEPTH):
        mod = silu_c @ w_ada[l] + b_ada[l]
        mod_c = silu_cc @ w_ada[l] + b_ada[l]
        x, xc = hybrid_layer(x, xc, mod, mod_c, norm_g[l], w_in[l], qa_g[l], kva_g[l],
                             w_uq[l], w_ukv[l], sgu_g[l], w_s[l], b_s[l], rpb[l], w_out[l],
                             ang_r, ang_c, l < DEPTH - 1)
    return rmsnorm(x, final_g)


_drawn_inputs = setup_inputs


def setup_inputs(seed=0):
    import zlib

    import numpy as np

    out = dict(_drawn_inputs(seed))
    spreads = {}
    factors = {'ctx': 3.305,
     'b_ada': 4.421,
     'norm_g': 8.0,
     'qa_g': 8.0,
     'kva_g': 8.0,
     'w_uq': 3.624,
     'sgu_g': 8.0,
     'b_s': 8.0,
     'rpb': 26.547,
     'final_g': 8.317}
    for name, (base, spread) in spreads.items():
        noise = np.random.default_rng([zlib.crc32(name.encode()), seed]).standard_normal(out[name].shape)
        drawn = base * np.exp(spread * noise) if base else spread * noise
        out[name] = __import__('jax').numpy.asarray(drawn.astype(out[name].dtype))
    for name, factor in factors.items():
        out[name] = (out[name] * factor).astype(out[name].dtype)
    return out
```

```python
from contextlib import ExitStack

import numpy as np

import concourse.bass as bass
from concourse import mybir

F32 = mybir.dt.float32
R32 = mybir.dt.float32r
I32 = mybir.dt.int32
ALU = mybir.AluOpType
ACT = mybir.ActivationFunctionType
AX = mybir.AxisListType

P = 128
D = 2048
KT = D // P
SEQ = CTX = 256
TOK = SEQ + CTX
DEPTH = 2
W_A, W_B, W_C = D // 4, D // 2, D // 4
HEADS_A, HEADS_B, HEADS_C = W_A // P, W_B // P, W_C // P
LORA = 512
KL = LORA // P
NOPE, ROPE = 128, 64
GRID_W = 64
ROWS = SEQ // GRID_W
IN_W = 3 * W_A + 2 * LORA + ROPE + W_B + 4 * W_C
EPS = 1e-6
MLA_SCALE = float((NOPE + ROPE) ** -0.5)
C_SCALE = float(P ** -0.5)
RPB_H, RPB_W = 15, 31
NEG = -1e30

COL = {}
_at = 0
for _n, _w in (("u", W_A), ("v_a", W_A), ("g_a", W_A), ("cq", LORA), ("ckv", LORA), ("kr", ROPE),
               ("g_b", W_B), ("q_c", W_C), ("k_c", W_C), ("v_c", W_C), ("g_c", W_C)):
    COL[_n] = _at
    _at += _w
assert _at == IN_W

RAW, RING, AHEAD = 8, 4, 3
FINAL_BANKS = (6, 7, 0, 1, 2, 3, 6, 7)
START_BLOCKS = 2 * D // 512
ADA_BLOCKS = 16
ADA_SLOTS = 4
ADA_BOTH = 12

C_ID, C_ROT, C_COS, C_SIN, C_TURN, C_KEEP, C_MASK, C_N = 0, 128, 256, 512, 768, 896, 960, 1024
Q_C, Q_NG, Q_QA, Q_KV, Q_BADA, Q_N = 0, 32, 64, 72, 80, 176


def query_tiles(l):
    return 4 if l < DEPTH - 1 else 2


def att_jobs(l, heads):
    out = []
    for h in range(heads):
        out.append((h, 0, 0))
        if l < DEPTH - 1:
            out.append((h, SEQ, SEQ))
    return out


def ada_vectors(block):
    return 2 if block < ADA_BOTH else 1


class Plan:

    def __init__(self):
        self.at = {}
        self.now = {"unit": 0, "job": 0, "ready": 0, "sq": 0, "att": 0, "ada": 0, **{b: 0 for b in range(8)}}
        add = self.add
        add("cols", 0, job=2, b={4: 1, 5: 1}, ready=2)
        add("x_t", 0, job=KT, b={6: KT // 2, 7: KT // 2}, sq=KT)
        add("start", 0, unit=KT * START_BLOCKS, job=START_BLOCKS, b={0: START_BLOCKS, 2: START_BLOCKS})
        for l in range(DEPTH):
            nt = query_tiles(l)
            jobs_c, jobs_b = len(att_jobs(l, HEADS_C)), len(att_jobs(l, HEADS_B))
            add("head", l, job=2, ready=1 + KT)
            add("v_c", l, unit=KT, b={0: 1, 1: 1, 2: 1, 3: 1})
            for n in ("q_c", "k_c", "g_c"):
                add(n, l, unit=16, b={0: 2, 1: 2})
                self.ada(l, n)
            add("att_c", l, att=jobs_c, b={6: jobs_c, 7: jobs_c, 2: (jobs_c + 1) // 2, 3: jobs_c // 2})
            add("v_a", l, unit=KT, b={i: 1 for i in range(nt)}, ready=1)
            add("w_s", l, job=1, ready=1)
            self.ada(l, "v_a")
            for n in ("u", "g_a"):
                add(n, l, unit=16, b={0: 2, 1: 2})
                self.ada(l, n)
            add("mix_a", l, job=4, b={2: 2, 3: 2}, ready=1)
            for n in ("cq", "ckv"):
                add(n, l, unit=16, b={0: 2, 1: 2}, sq=4)
                self.ada(l, n)
            add("lat", l, job=3, ready=2)
            add("kr", l, unit=4, job=1, b={2: 1, 3: 1})
            add("latn", l, ready=2 * KL)
            add("krn", l, ready=2)
            add("g_b", l, unit=32, b={0: 4, 1: 4})
            self.ada(l, "g_b")
            add("v_b", l, unit=8, b={0: 2, 1: 2, 2: 2, 3: 2})
            add("q_r", l, unit=4, job=4, b={0: 2, 1: 2, 2: 2, 3: 2}, ready=4)
            add("heads", l, unit=2 * HEADS_B, att=jobs_b,
                b={0: HEADS_B, 1: HEADS_B, 6: jobs_b, 7: jobs_b,
                   2: (jobs_b + 1) // 2, 3: jobs_b // 2})
            for n in ("out1", "out3", "out5"):
                self.ada(l, n)
            add("out", l, unit=64, ready=KT, b={0: 8, 1: 8}, sq=KT)
        add("end", 0)
        assert self.now["ada"] == ADA_BLOCKS

    def add(self, name, l, b=None, **more):
        self.at[name, l] = dict(self.now)
        for k, v in {**(b or {}), **more}.items():
            self.now[k] += v

    ADA_IN = {0: ("q_c", "k_c", "g_c", "v_a", "u", "g_a", "cq", "ckv", "g_b", "out1", "out3", "out5"),
              1: ("k_c", "u", "g_a", "ckv")}

    def ada(self, l, after):
        if after in self.ADA_IN[l]:
            self.add(("ada", after), l, b={6: 1, 7: ada_vectors(self.now["ada"]) - 1}, ada=1)

    def __getitem__(self, key):
        return self.at[key]


PLAN = Plan()


def ada_steps(block):
    return (KT + 1) * (2 * min(block, ADA_BOTH) + max(0, block - ADA_BOTH))
UNITS = PLAN["end", 0]["unit"]


KR_UNITS = [PLAN["kr", l]["unit"] + q for l in range(DEPTH) for q in range(4)]


def twice(dst, src):
    return (dst.rearrange("p (k t n) -> p k t n", k=4, t=2),
            src.rearrange("p (k n) -> p k n", k=4)[:, :, 0:ROPE].unsqueeze(2).broadcast_to([P, 4, 2, ROPE]))


def raw_extra(u):
    two = [PLAN["q_r", l]["unit"] + i for l in range(DEPTH) for i in range(4)]
    return 16 * sum(1 for t in two if t <= u and t % RAW == u % RAW)


def hybrid_kernel(nc, x, ctx_in, w_ada, w_in, w_uq, w_ukv, sgu_g, w_s, b_s, rpb, w_out, final_g,
                  rows_a, rows_b, consts, out):
    x_scratch = nc.dram_tensor("x_scratch", (P, KT, TOK), F32).ap()

    with ExitStack() as stack:
        def sem(name):
            return stack.enter_context(nc.semaphore(name))

        stack.enter_context(nc.sbuf_tensor("arena", [P, 207 * 256], F32))
        base = (16481 + 31) // 32 * 32

        def at(name, kib, shape, dt=F32):
            return nc.alloc_sbuf_tensor_at(name, [P, *shape], dt, offset=base + int(kib * 1024))

        h_hi, h_lo = at("h_hi", 0, [KT, TOK], R32), at("h_lo", 32, [KT, TOK], R32)
        c_st = at("c_st", 0, [KT, P], R32)
        x_in = at("x_in", 32, [4, D])
        v_hi, v_lo = at("v_hi", 0, [4, W_B], R32), at("v_lo", 32, [4, W_B], R32)
        qr_hi, qr_lo = at("qr_hi", 16, [4, TOK], R32), at("qr_lo", 48, [4, TOK], R32)
        qk_hi, qk_lo = at("qk_hi", 24, [4, TOK], R32), at("qk_lo", 56, [4, TOK], R32)
        z = at("z", 64, [KT, TOK])
        kc_hi, kc_lo = at("kc_hi", 64, [4, TOK], R32), at("kc_lo", 72, [4, TOK], R32)
        VA, UG, RAWL = 4, 8, 4
        vc_hi, vc_lo = at("vc_hi", 96, [4, W_C], R32), at("vc_lo", 104, [4, W_C], R32)
        qc_hi, qc_lo = at("qc_hi", 112, [4, TOK], R32), at("qc_lo", 120, [4, TOK], R32)
        cv_hi, cv_lo = at("cv_hi", 96, [KL, TOK], R32), at("cv_lo", 104, [KL, TOK], R32)
        cq_hi, cq_lo = at("cq_hi", 112, [KL, TOK], R32), at("cq_lo", 120, [KL, TOK], R32)
        kr_ab = at("kr_ab", 128, [4, TOK], R32)
        ptc_hi, ptc_lo = at("ptc_hi", 128, [4, 256], R32), at("ptc_lo", 132, [4, 256], R32)
        y = at("y", 96, [2, D])
        fg_row = at("fg_row", 112, [D])
        w_raw = at("w_raw", 136, [RAW, 512])
        w_hi, w_lo = at("w_hi", 152, [RING, 512], R32), at("w_lo", 160, [RING, 512], R32)
        ada_w = at("ada_w", 168, [ADA_SLOTS, 512])
        ada_acc = at("ada_acc", 176, [2, 512])
        bias = at("bias", 180, [8, 256])
        bs_row, sgu_row = at("bs_row", 180, [4, P]), at("sgu_row", 182, [W_A])
        ws_t, ws_in = at("ws_t", 184, [4, P]), at("ws_in", 186, [4, P])
        ptb_hi, ptb_lo = at("ptb_hi", 180, [4, 256], R32), at("ptb_lo", 184, [4, 256], R32)
        x_res = at("x_res", 180, [2, TOK])
        prob = at("prob", 188, [2, TOK])
        tmp = at("tmp", 192, [4, TOK])
        cst = at("cst", 200, [C_N])
        ones = at("ones", 204.0, [P])
        cols = at("cols", 204.5, [Q_N])
        mods = at("mods", 205.25, [2, 96])
        c_silu = at("c_silu", 206.0, [32])
        a_col = at("a_col", 206.125, [2, KT])
        small = at("small", 206.25, [60])
        ident, rot = cst[:, C_ID:C_ID + P], cst[:, C_ROT:C_ROT + P]
        turn_rows = cst[:, C_TURN:C_TURN + P]
        cos, sin = cst[:, C_COS:C_COS + SEQ], cst[:, C_SIN:C_SIN + SEQ]

        ps = stack.enter_context(nc.psum_tensor("ps", [P, 8, 512], F32))

        raw_in = [sem(f"raw_in{i}") for i in range(RAW)]
        hi_made, lo_made = sem("hi_made"), sem("lo_made")
        unit_done = sem("unit_done")
        free = [sem(f"free{b}") for b in range(8)]
        job_done = sem("job_done")
        op_hi = sem("op_hi")
        op_ready = sem("op_ready")
        t_ready = sem("t_ready")
        sq_ready, sq_sum = sem("sq_ready"), sem("sq_sum")
        scores_done, nmax_ready, exp_done = sem("scores_done"), sem("nmax_ready"), sem("exp_done")
        prob_ready, prob_turned, av_done = sem("prob_ready"), sem("prob_turned"), sem("av_done")
        dve_step, act_step, pool_step = sem("dve_step"), sem("act_step"), sem("pool_step")
        rows_in, const_in, x_landed = sem("rows_in"), sem("const_in"), sem("x_landed")
        bias_in, gate_in, fg_in = sem("bias_in"), sem("gate_in"), sem("fg_in")
        bias_ready, pool_set = sem("bias_ready"), sem("pool_set")
        ada_in = [sem(f"ada_in{i}") for i in range(ADA_SLOTS)]
        ada_step = sem("ada_step")
        ada_taken = sem("ada_taken")
        x_kept, x_back = sem("x_kept"), [sem("x_back0"), sem("x_back1")]
        out_stored = sem("out_stored")

        block = stack.enter_context(nc.Block())

        @block.sync
        def _(sp):
            sp.dma_start(tmp[0:80, 0, 0:P], rows_a).then_inc(rows_in, 16)
            sp.dma_start(tmp[0:96, 1, 0:P], rows_b).then_inc(rows_in, 16)
            sp.dma_start(cst[:, :], consts).then_inc(const_in, 16)
            for t in range(2):
                sp.dma_start(x_in[:, t, :], x[0, t * P:(t + 1) * P, :]).then_inc(x_landed, 16)
                sp.dma_start(x_in[:, 2 + t, :], ctx_in[0, t * P:(t + 1) * P, :]).then_inc(x_landed, 16)

            def slot_free(u, i=0, per=0):
                if u >= RAW:
                    sp.wait_ge(lo_made, u - RAW + 1 + per * i)

            def load_bias(l):
                for h in range(HEADS_C):
                    for r in range(ROWS):
                        src = bass.AP(tensor=rpb.tensor,
                                      offset=((l * HEADS_C + h) * RPB_H + 7 - r) * RPB_W + 15 - (GRID_W - 1),
                                      ap=[[1, GRID_W], [RPB_W, ROWS], [1, GRID_W]])
                        q0 = GRID_W * (r % 2)
                        sp.dma_start(bias[q0:q0 + GRID_W, 2 * h + r // 2, :].rearrange("p (r c) -> p r c", r=ROWS),
                                     src).then_inc(bias_in, 16)

            def tile_units(src3, u, i, j, q):
                un = u + 4 * j + q
                slot_free(un, i, 8)
                sp.dma_start(w_raw[:, un % RAW, :].rearrange("p (k n) -> p k n", k=4),
                             src3[:, 4 * q:4 * q + 4, bass.ds((2 * i + j) * P, P)]).then_inc(raw_in[un % RAW], 16)

            def tiles(w2, col, width, u):
                src3 = w2[:, col:col + width].rearrange("(k p) n -> p k n", p=P)
                with sp.Fori(0, width // (2 * P)) as i:
                    for j in range(2):
                        for q in range(4):
                            tile_units(src3, u, i, j, q)

            def rows(w2, col, u, n=KT, k0=0):
                for k in range(k0, n):
                    slot_free(u + k)
                    sp.dma_start(w_raw[:, (u + k) % RAW, :], w2[k * P:(k + 1) * P, col:col + 512])\
                        .then_inc(raw_in[(u + k) % RAW], 16)

            load_bias(0)
            def ada_row(k, b):
                sp.dma_start(w_raw[:, k % RAW, :], w_ada[0, k * P:(k + 1) * P, bass.ds(512 * b, 512)])\
                    .then_inc(raw_in[k % RAW], 16)

            for k in range(RAW):
                ada_row(k, 0)
            with sp.Fori(0, START_BLOCKS - 1) as b:
                for k in range(KT):
                    sp.wait_ge(lo_made, k + 1 + KT * b)
                    ada_row((RAW + k) % KT, b + (RAW + k) // KT)
            for k in range(KT - RAW, KT):
                slot_free(KT * (START_BLOCKS - 1) + k)
                ada_row(k, START_BLOCKS - 1)

            for l in range(DEPTH):
                w2 = w_in[l]
                nq = query_tiles(l) * P
                rows(w2, COL["v_c"], PLAN["v_c", l]["unit"], k0=0 if l == 0 else AHEAD)
                if l == 0:
                    sp.wait_ge(free[7], KT // 2)
                    sp.wait_ge(free[6], KT // 2)
                    sp.dma_start(x_scratch, z[:, :, :]).then_inc(x_kept, 16)
                else:
                    load_bias(l)
                for n in ("q_c", "k_c", "g_c"):
                    tiles(w2, COL[n], 512, PLAN[n, l]["unit"])
                u = PLAN["v_a", l]["unit"]
                rows(w2, COL["v_a"], u, 8)
                j = PLAN["v_a", l]["att"]
                sp.wait_ge(av_done, j)
                sp.dma_start(bs_row[:, :, :], b_s[l:l + 1].broadcast_to([P, HEADS_A, P])).then_inc(gate_in, 16)
                sp.dma_start(sgu_row[:, :], sgu_g[l:l + 1, :].broadcast_to([P, W_A])).then_inc(gate_in, 16)
                sp.dma_start(ws_in[:, :, :], w_s[l].rearrange("g p q -> p g q")).then_inc(gate_in, 16)
                rows(w2, COL["v_a"], u, KT, 8)
                for n in ("u", "g_a", "cq", "ckv"):
                    tiles(w2, COL[n], 512, PLAN[n, l]["unit"])
                u = PLAN["kr", l]["unit"]
                src3 = w2[:, COL["kr"]:COL["kr"] + ROPE].rearrange("(k p) n -> p k n", p=P)
                for q in range(4):
                    slot_free(u + q)
                    dst = w_raw[:, (u + q) % RAW, :].rearrange("p (k n) -> p k n", k=4)
                    sp.dma_start(dst[:, :, 0:ROPE], src3[:, 4 * q:4 * q + 4, :]).then_inc(raw_in[(u + q) % RAW], 16)
                tiles(w2, COL["g_b"], W_B, PLAN["g_b", l]["unit"])

                u = PLAN["v_b", l]["unit"]
                for half in range(2):
                    src = w_ukv[l].rearrange("k (h n) -> k h n", h=HEADS_B)[:, 4 * half:4 * half + 4, NOPE:]
                    for k in range(KL):
                        un = u + 4 * half + k
                        slot_free(un)
                        sp.dma_start(w_raw[:, un % RAW, :].rearrange("p (h n) -> p h n", h=4),
                                     src[k * P:(k + 1) * P]).then_inc(raw_in[un % RAW], 16)
                u = PLAN["q_r", l]["unit"]
                uq3 = w_uq[l].rearrange("(k p) (h n) -> p k h n", p=P, h=HEADS_B)
                for pair in range(4):
                    slot_free(u + pair)
                    dst = w_raw[:, (u + pair) % RAW, :].rearrange("p (k n) -> p k n", k=4)
                    for half in range(2):
                        sp.dma_start(dst[:, :, half * ROPE:(half + 1) * ROPE], uq3[:, :, 2 * pair + half, NOPE:])\
                            .then_inc(raw_in[(u + pair) % RAW], 16)
                ukv3 = w_ukv[l].rearrange("(k p) (h n) -> p k h n", p=P, h=HEADS_B)
                u = PLAN["heads", l]["unit"]
                for h in range(HEADS_B):
                    for m, src in enumerate((uq3[:, :, h, 0:NOPE], ukv3[:, :, h, 0:NOPE])):
                        un = u + 2 * h + m
                        slot_free(un)
                        sp.dma_start(w_raw[:, un % RAW, :].rearrange("p (k n) -> p k n", k=4), src)\
                            .then_inc(raw_in[un % RAW], 16)

                p = PLAN["out", l]
                u, f0 = p["unit"], p[0]
                src3 = w_out[l].rearrange("(k p) n -> p k n", p=P)
                for q in range(8):
                    un = u + q
                    slot_free(un)
                    sp.dma_start(w_raw[:, un % RAW, :].rearrange("p (k n) -> p k n", k=4),
                                 src3[:, 4 * (q % 4):4 * (q % 4) + 4, (q // 4) * P:(q // 4 + 1) * P])\
                        .then_inc(raw_in[un % RAW], 16)
                sp.wait_ge(x_kept, 16 if l == 0 else 16 * (1 + KT))
                sp.wait_ge(av_done, p["att"])
                for j in range(2):
                    sp.dma_start(x_res[:, j, 0:nq], x_scratch[:, j, 0:nq]).then_inc(x_back[j], 16)
                with sp.Fori(1, KT // 2) as i:
                    for j in range(2):
                        for q in range(4):
                            un = u + 4 * j + q
                            sp.wait_ge(lo_made, un - RAW + 1 + 8 * i)
                            sp.dma_start(w_raw[:, un % RAW, :].rearrange("p (k n) -> p k n", k=4),
                                         src3[:, 4 * q:4 * q + 4, bass.ds((2 * i + j) * P, P)])\
                                .then_inc(raw_in[un % RAW], 16)
                        sp.wait_ge(free[j], p[j] + i)
                        if l == 0:
                            sp.dma_start(x_scratch[:, bass.ds(2 * i + j - 2, 1), :], z[:, bass.ds(2 * i + j - 2, 1), :])\
                                .then_inc(x_kept, 16)
                        sp.dma_start(x_res[:, j, 0:nq], x_scratch[:, bass.ds(2 * i + j, 1), 0:nq]).then_inc(x_back[j], 16)
                if l == 0:
                    rows(w_in[1], COL["v_c"], PLAN["v_c", 1]["unit"], AHEAD)
                    for j in range(2):
                        sp.wait_ge(free[j], p[j] + 8)
                        sp.dma_start(x_scratch[:, KT - 2 + j, :], z[:, KT - 2 + j, :]).then_inc(x_kept, 16)
                else:
                    sp.dma_start(fg_row[:, :], final_g.rearrange("(a n) -> a n", a=1).broadcast_to([P, D]))\
                        .then_inc(fg_in, 16)
            for g in range(4):
                tt, c0 = g // 2, (g % 2) * 1024
                for n in (2 * g, 2 * g + 1):
                    b = FINAL_BANKS[n]
                    sp.wait_ge(free[b], PLAN["end", 0][b] + FINAL_BANKS[:n + 1].count(b))
                sp.dma_start(out[0, tt * P:(tt + 1) * P, c0:c0 + 1024], y[:, tt, c0:c0 + 1024]).then_inc(out_stored, 16)
            sp.wait_ge(out_stored, 64)

        @block.gpsimd
        def _(pool):
            pool.memset(ones[:, :], 1.0).then_inc(pool_set, 1)
            pool.memset(c_st[:, :, :].bitcast(F32), 0.0).then_inc(pool_set, 1)
            keep = cst[:, C_KEEP:C_KEEP + GRID_W].unsqueeze(1).broadcast_to([P, 32, GRID_W])
            mask = cst[:, C_MASK:C_MASK + GRID_W].unsqueeze(1).broadcast_to([P, 32, GRID_W])
            steps = [0]

            def mask_bias(l):
                v = bias[:, :, :].rearrange("p a (r c) -> p (a r) c", c=GRID_W)
                pool.wait_ge(bias_in, 16 * ROWS * HEADS_C * (l + 1))
                pool.tensor_tensor(v, v, keep, ALU.mult).then_inc(bias_ready, 1)
                pool.wait_ge(bias_ready, 2 * l + 1)
                pool.tensor_tensor(v, v, mask, ALU.add).then_inc(bias_ready, 1)

            pool.wait_ge(const_in, 16)
            mask_bias(0)
            pool.wait_ge(unit_done, KT * START_BLOCKS - RAW)

            def ada_rows(l, first, count, col):
                vectors, n0 = ada_vectors(first), ada_steps(first)

                def load(b, k):
                    pool.dma_start(ada_w[:, k % ADA_SLOTS, :],
                                   w_ada[l, k * P:(k + 1) * P, bass.ds(col + 512 * b, 512)])\
                        .then_inc(ada_in[k % ADA_SLOTS], 16)

                for k in range(KT):
                    if k >= ADA_SLOTS or first:
                        before = n0 + vectors * (k + 1 - ADA_SLOTS + 1)
                        if k < ADA_SLOTS:
                            before = n0 - ada_vectors(first - 1) * (ADA_SLOTS - 1 - k)
                        pool.wait_ge(ada_step, before)
                    load(0, k)
                with pool.Fori(1, count) as b:
                    n = n0 + vectors * (KT + 1) * b
                    for k in range(KT):
                        used = vectors * (k + 2 - ADA_SLOTS) if k >= ADA_SLOTS else -vectors * (ADA_SLOTS - 1 - k)
                        pool.wait_ge(ada_step, n + used)
                        load(b, k)

            ada_rows(0, 0, 4, 2 * D)
            ada_rows(1, 4, 8, 0)
            mask_bias(1)
            ada_rows(1, 12, 4, 2 * D)

        @block.scalar
        def _(act):
            hi_n, t_n, sq_n, a_n = [0], [0], [0], [0]

            def prep(u, i=0, per=0):
                act.wait_ge(raw_in[u % RAW], 16 * (u // RAW + 1) + raw_extra(u) + 16 * (per // RAW) * i)
                if u >= RING or per:
                    act.wait_ge(unit_done, u - RING + 1 + per * i)
                dst, src = w_hi[:, u % RING, :], w_raw[:, u % RAW, :]
                if per == 0 and u in KR_UNITS:
                    dst, src = twice(dst, src)
                act.activation(dst, src, ACT.Copy).then_inc(hi_made, 1)

            def prep_ahead(u, i=0, per=0):
                if u + AHEAD < UNITS:
                    prep(u + AHEAD, i, per)

            def hi(dst, src, scale=1.0):
                hi_n[0] += 1
                act.activation(dst, src, ACT.Copy, scale=scale).then_inc(op_hi, 1)

            def tiles(name, l, evac, count=4, start=0):
                p = PLAN[name, l]
                u = p["unit"]

                def turn(i, u, per):
                    for s in range(8):
                        if s == 4:
                            evac(i, 0)
                        prep_ahead(u + s, i, per)
                    evac(i, 1)

                n = count // 2 - (name == "ckv")
                with act.Fori(start, n) as i:
                    turn(i, u, 8)
                if n < count // 2:
                    turn(n, u + 8 * n, 0)

            def tile_full(p, i, j):
                act.wait_ge(unit_done, p["unit"] + 4 * (j + 1) + 8 * i)

            act.wait_ge(free[4], 1)
            act.activation(c_silu[:, :], cols[:, Q_C:Q_C + 32], ACT.Silu).then_inc(act_step, 1)
            act.wait_ge(act_step, 1)
            act.wait_ge(pool_set, 2)
            for v in range(2):
                hi(c_st[:, :, 2 * v], c_silu[:, v * KT:(v + 1) * KT])

            for t in range(KT):
                act.wait_ge(job_done, PLAN["x_t", 0]["job"] + t + 1)
                if t >= 2:
                    act.wait_ge(sq_sum, t - 1)
                act.activation(tmp[:, t % 2, :], ps[:, 6 + t % 2, :], ACT.Square).then_inc(sq_ready, 1)
                act.activation(z[:, t, :], ps[:, 6 + t % 2, :], ACT.Copy).then_inc(free[6 + t % 2], 1)
            sq_n[0] = KT

            for u in range(AHEAD):
                prep(u)

            def start_block(b, per):
                for k in range(KT):
                    prep(k + AHEAD, b, per)
                act.wait_ge(unit_done, KT + KT * b)
                act.activation(tmp[0:4, 3, :], ps[0:4, 0, :], ACT.Copy).then_inc(free[0], 1)

            start_block(0, 0)
            with act.Fori(1, START_BLOCKS) as b:
                start_block(b, KT)

            def softmax_exp(j, keys):
                for qt in range(2):
                    n = 2 * j + qt
                    act.wait_ge(nmax_ready, n + 1)
                    if n >= 2:
                        act.wait_ge(prob_turned, n - 1)
                    act.activation(prob[:, qt, 0:keys], ps[:, 4 + qt, 0:keys], ACT.Exp, bias=small[:, 40 + qt:41 + qt],
                                   accum_out=small[:, 42 + qt:43 + qt]).then_inc(exp_done, 1)

            def turned_hi(j, keys, pt):
                nk = keys // P
                if j >= 1:
                    act.wait_ge(av_done, j)
                for qt in range(2):
                    act.wait_ge(prob_turned, 2 * j + qt + 1)
                    hi(pt[:, 0:nk, qt * P:(qt + 1) * P],
                       ps[:, 6 + qt, 0:keys].rearrange("p (k q) -> p k q", k=nk))

            for l in range(DEPTH):
                nt = query_tiles(l)
                nq = nt * P
                u = PLAN["v_c", l]["unit"]
                for k in range(KT):
                    t_n[0] += 1
                    act.wait_ge(t_ready, t_n[0])
                    for v in range(2):
                        hi_n[0] += v
                        ins = act.activation(h_hi[:, k, v * SEQ:(v + 1) * SEQ], tmp[:, k % 2, v * SEQ:(v + 1) * SEQ],
                                             ACT.Identity, bias=mods[:, v, 48 * l + k:48 * l + k + 1])
                    ins.then_inc(op_hi, 1)
                    if k >= 2:
                        prep_ahead(u + k - 2)
                prep_ahead(u + KT - 2)
                prep_ahead(u + KT - 1)

                act.wait_ge(unit_done, u + KT)
                for tt in range(4):
                    hi(vc_hi[:, tt, :], ps[:, tt, :])
                act.wait_ge(x_kept, 16 * (1 + KT * l))

                def q_tile(i, j):
                    tile_full(PLAN["q_c", l], i, j)
                    act.activation(qc_hi[:, bass.ds(2 * i + j, 1), 0:nq], ps[:, j, 0:nq], ACT.Copy, scale=C_SCALE)\
                        .then_inc(op_hi, 1)

                def k_tile(i, j):
                    tile_full(PLAN["k_c", l], i, j)
                    act.activation(kc_hi[:, bass.ds(2 * i + j, 1), :], ps[:, j, :], ACT.Copy).then_inc(op_hi, 1)

                def gate_tile(name, first, func=ACT.Silu):
                    def evac(i, j):
                        tile_full(PLAN[name, l], i, j)
                        act.activation(z[:, bass.ds(first + 2 * i + j, 1), 0:nq], ps[:, j, 0:nq], func)\
                            .then_inc(free[j], 1)
                    return evac

                tiles("q_c", l, q_tile)
                tiles("k_c", l, k_tile)
                hi_n[0] += 8
                tiles("g_c", l, gate_tile("g_c", 12))

                jobs = att_jobs(l, HEADS_C)
                j0 = PLAN["att_c", l]["att"]
                for r in range(-1, len(jobs)):
                    if r + 1 < len(jobs):
                        _, q0, k0 = jobs[r + 1]
                        softmax_exp(j0 + r + 1, TOK - k0)
                    if r >= 0:
                        turned_hi(j0 + r, TOK - jobs[r][2], ptc_hi)

                u = PLAN["v_a", l]["unit"]
                for k in range(KT):
                    prep_ahead(u + k)
                act.wait_ge(unit_done, u + KT)
                for tt in range(nt):
                    act.activation(z[:, VA + tt, :], ps[:, tt, :], ACT.Gelu_apprx_tanh).then_inc(free[tt], 1)
                tiles("u", l, gate_tile("u", UG, ACT.Gelu_apprx_tanh))
                tiles("g_a", l, gate_tile("g_a", 0))

                def raw_tile(name, first, n):
                    sq0 = sq_n[0]
                    def evac(i, j):
                        tile_full(PLAN[name, l], i, j)
                        act.wait_ge(sq_sum, sq0 + j - 1 + 2 * i)
                        act.activation(tmp[:, j, 0:n], ps[:, j, 0:n], ACT.Square).then_inc(sq_ready, 1)
                        act.activation(z[:, bass.ds(first + 2 * i + j, 1), 0:n], ps[:, j, 0:n], ACT.Copy)\
                            .then_inc(free[j], 1)
                    return evac

                act.wait_ge(op_ready, PLAN["cq", l]["ready"])
                tiles("cq", l, raw_tile("cq", RAWL, nq))
                sq_n[0] += 4
                tiles("ckv", l, raw_tile("ckv", RAWL + KL, TOK))
                sq_n[0] += 4

                p = PLAN["kr", l]
                for q in range(4):
                    prep_ahead(p["unit"] + q)
                act.wait_ge(unit_done, p["unit"] + 4)
                act.activation(prob[:, 0, :], ps[:, 2, :], ACT.Copy).then_inc(free[2], 1)

                u = PLAN["g_b", l]["unit"]
                g_b = gate_tile("g_b", 4)
                for s in range(8):
                    t_n[0] += 1
                    act.wait_ge(t_ready, t_n[0])
                    n = nq if s < KL else TOK
                    hi((cq_hi if s < KL else cv_hi)[:, s % KL, 0:n], tmp[:, 2 + s % 2, 0:n])
                    if s == 4:
                        g_b(0, 0)
                    prep_ahead(u + s)
                t_n[0] += 1
                act.wait_ge(t_ready, t_n[0])
                hi(kr_ab[0:ROPE, 0, :], prob[0:ROPE, 0, :])
                hi(kr_ab[ROPE:P, 2, :], prob[ROPE:P, 0, :])
                g_b(0, 1)
                tiles("g_b", l, g_b, 8, 1)

                u = PLAN["v_b", l]["unit"]
                for half in range(2):
                    for k in range(KL):
                        prep_ahead(u + 4 * half + k)
                    act.wait_ge(unit_done, u + 4 * half + 4)
                    for tt in range(4):
                        hi(v_hi[:, tt, half * 512:half * 512 + 512], ps[:, tt, :])

                u = PLAN["q_r", l]["unit"]
                t0 = t_n[0]
                for pair in range(5):
                    if pair < 4:
                        prep_ahead(u + pair)
                        act.wait_ge(unit_done, u + pair + 1)
                        if pair >= 2:
                            act.wait_ge(t_ready, t0 + pair - 1)
                        act.activation(prob[:, pair % 2, 0:nq], ps[:, pair % 2, 0:nq], ACT.Copy)\
                            .then_inc(free[pair % 2], 1)
                    if pair >= 1:
                        t_n[0] += 1
                        act.wait_ge(t_ready, t_n[0])
                        hi(qr_hi[:, pair - 1, 0:nq], tmp[:, 2 + (pair - 1) % 2, 0:nq])

                u = PLAN["heads", l]["unit"]

                def head_operands(h):
                    prep_ahead(u + 2 * h)
                    act.wait_ge(unit_done, u + 2 * h + 1)
                    hi(qk_hi[:, h % 2, 0:nq], ps[:, 0, 0:nq], MLA_SCALE)
                    prep_ahead(u + 2 * h + 1)
                    act.wait_ge(unit_done, u + 2 * h + 2)
                    hi(qk_hi[:, 2 + h % 2, :], ps[:, 1, :])

                jobs = att_jobs(l, HEADS_B)
                j0 = PLAN["heads", l]["att"]
                head_operands(0)
                for r in range(-1, len(jobs)):
                    if r + 1 < len(jobs):
                        h, q0, k0 = jobs[r + 1]
                        if q0 == 0 and h + 1 < HEADS_B:
                            head_operands(h + 1)
                        softmax_exp(j0 + r + 1, TOK - k0)
                    if r >= 0:
                        turned_hi(j0 + r, TOK - jobs[r][2], ptb_hi)

                p = PLAN["out", l]
                u = p["unit"]
                last = p["att"] - 1 - j0
                act.wait_ge(free[2 + last % 2], p[2 + last % 2])
                sq0 = sq_n[0]

                def new_x(i, j):
                    act.wait_ge(free[j], p[j] + 1 + i)
                    act.wait_ge(sq_sum, sq0 + j - 1 + 2 * i)
                    act.activation(tmp[:, j, 0:nq], z[:, bass.ds(2 * i + j, 1), 0:nq], ACT.Square).then_inc(sq_ready, 1)

                for t in range(KT):
                    hi(h_hi[:, t, 0:nq], z[:, t, 0:nq])
                    if t % 4 == 3:
                        prep_ahead(u + t // 4)
                for s in range(4, 8):
                    prep_ahead(u + s)
                    if s == 5:
                        new_x(0, 0)
                if l == 0:
                    with act.Fori(1, KT // 2) as i:
                        for s in range(8):
                            if s == 1:
                                new_x(i - 1, 1)
                            if s == 5:
                                new_x(i, 0)
                            prep_ahead(u + s, i, 8)
                else:
                    with act.Fori(1, KT // 2 - 1) as i:
                        for s in range(8):
                            if s == 1:
                                new_x(i - 1, 1)
                            if s == 5:
                                new_x(i, 0)
                            prep_ahead(u + s, i, 8)
                    i = KT // 2 - 1
                    for s in range(8):
                        if s == 1:
                            new_x(i - 1, 1)
                        if s == 5:
                            new_x(i, 0)
                        prep_ahead(u + 8 * i + s)
                new_x(KT // 2 - 1, 1)
                sq_n[0] += KT

        @block.tensor
        def _(pe):
            def wait_unit(u, i=0, per=0):
                pe.wait_ge(lo_made, u + 1 + per * i)

            def split_mm(dst, a_hi, a_lo, b_hi, b_lo, first, last):
                pe.matmul(dst, a_lo, b_hi, start=first, stop=False)
                pe.matmul(dst, a_hi, b_lo, start=False, stop=False)
                return pe.matmul(dst, a_hi, b_hi, start=False, stop=last)

            def turn(dst, src, n=P):
                return pe.transpose(dst, src, ident[0:n, 0:n])

            def stationary_unit(dst, u, b_hi, b_lo, k0, cols_n, first, last):
                s = u % RING
                for kk in range(4):
                    w = slice(kk * P, (kk + 1) * P)
                    mm = split_mm(dst, w_hi[:, s, w], w_lo[:, s, w], b_hi[:, k0 + kk, 0:cols_n],
                                  b_lo[:, k0 + kk, 0:cols_n], first and kk == 0, last and kk == 3)
                mm.then_inc(unit_done, 1)

            def tiles(name, l, n, count=4):
                p = PLAN[name, l]
                u = p["unit"]
                with pe.Fori(0, count // 2) as i:
                    for j in range(2):
                        pe.wait_ge(free[j], p[j] + i)
                        for q in range(4):
                            wait_unit(u + 4 * j + q, i, 8)
                            stationary_unit(ps[:, j, 0:n], u + 4 * j + q, h_hi, h_lo, 4 * q, n, q == 0, q == 3)

            def moving_unit(u, a_hi, a_lo, k, nt, first, last):
                s = u % RING
                for tt in range(nt):
                    t = slice(tt * P, (tt + 1) * P)
                    mm = split_mm(ps[:, tt, :], a_hi[:, k, t], a_lo[:, k, t], w_hi[:, s, :], w_lo[:, s, :], first, last)
                mm.then_inc(unit_done, 1)

            def ada(l, after):
                if (("ada", after), l) not in PLAN.at:
                    return
                p = PLAN[("ada", after), l]
                pe.wait_ge(ada_step, ada_steps(p["ada"] + 1))
                for v in range(ada_vectors(p["ada"])):
                    pe.wait_ge(free[6 + v], p[6 + v])
                    for c in range(4):
                        mm = turn(ps[:, 6 + v, c * P:(c + 1) * P], ada_acc[:, v, c * P:(c + 1) * P])
                mm.then_inc(ada_taken, 1)

            pe.wait_ge(const_in, 16)
            pe.wait_ge(rows_in, 32)
            turn(ps[:, 4, 0:80], tmp[0:80, 0, 0:P], 80).then_inc(job_done, 1)
            turn(ps[:, 5, 0:96], tmp[0:96, 1, 0:P], 96).then_inc(job_done, 1)
            pe.wait_ge(x_landed, 64)
            for t in range(KT):
                if t >= 2:
                    pe.wait_ge(free[6 + t % 2], t // 2)
                for tt in range(4):
                    mm = turn(ps[:, 6 + t % 2, tt * P:(tt + 1) * P], x_in[:, tt, t * P:(t + 1) * P])
                mm.then_inc(job_done, 1)

            pe.wait_ge(op_ready, 2)
            with pe.Fori(0, START_BLOCKS) as b:
                for k in range(KT):
                    wait_unit(k, b, KT)
                    pe.matmul(ps[:, 0, :], c_st[:, k, :], w_lo[:, k % RING, :], start=k == 0, stop=False)
                    mm = pe.matmul(ps[:, 0, :], c_st[:, k, :], w_hi[:, k % RING, :], start=False, stop=k == KT - 1)
                    mm.then_inc(unit_done, 1)
                pe.wait_ge(free[0], b + 1)
                for c in range(4):
                    mm = pe.matmul(ps[:, 2, 4 * c:4 * c + 4], tmp[0:4, 3, c * P:(c + 1) * P], ident[0:4, 0:4],
                                   start=True, stop=True)
                mm.then_inc(job_done, 1)
                pe.wait_ge(free[2], b + 1)

            for l in range(DEPTH):
                nt = query_tiles(l)
                nq = nt * P
                p = PLAN["head", l]
                pe.wait_ge(sq_sum, p["sq"])
                for c in range(4):
                    mm = pe.matmul(ps[:, 4, c:c + 1], tmp[:, 2, c * P:(c + 1) * P], ones[:, 0:1], start=True, stop=True)
                mm.then_inc(job_done, 1)
                pe.wait_ge(op_ready, p["ready"] + 1)
                pe.matmul(ps[:, 5, :], ones[:, :], tmp[:, 3, :], start=True, stop=True).then_inc(job_done, 1)

                u = PLAN["v_c", l]["unit"]
                for k in range(KT):
                    wait_unit(u + k)
                    pe.wait_ge(op_ready, p["ready"] + 2 + k)
                    if k == 0:
                        for tt in range(4):
                            pe.wait_ge(free[tt], PLAN["v_c", l][tt])
                    moving_unit(u + k, h_hi, h_lo, k, 4, k == 0, k == KT - 1)
                for n, w in (("q_c", nq), ("k_c", TOK), ("g_c", nq)):
                    tiles(n, l, w)
                    ada(l, n)

                def scores(j, terms, keys, bias_of=None):
                    for qt in range(2):
                        if j >= 1:
                            pe.wait_ge(exp_done, 2 * j + qt - 1)
                        for n, (qh, ql, kh, kl, q0, k0) in enumerate(terms):
                            q = slice(q0 + qt * P, q0 + (qt + 1) * P)
                            k, dst = slice(k0, k0 + keys), ps[:, 4 + qt, 0:keys]
                            pe.matmul(dst, ql[:, q], kh[:, k], start=n == 0, stop=False)
                            if bias_of is not None:
                                pe.matmul(ps[:, 4 + qt, 0:SEQ], turn_rows, bias[:, 2 * bias_of + qt, :],
                                          start=False, stop=False)
                            pe.matmul(dst, qh[:, q], kl[:, k], start=False, stop=False)
                            mm = pe.matmul(dst, qh[:, q], kh[:, k], start=False, stop=n == len(terms) - 1)
                        mm.then_inc(scores_done, 1)

                def turn_probs(p, r, keys):
                    for qt in range(2):
                        pe.wait_ge(prob_ready, 2 * (p["att"] + r) + qt + 1)
                        pe.wait_ge(free[6 + qt], p[6 + qt] + r)
                        for c in range(keys // P):
                            mm = turn(ps[:, 6 + qt, c * P:(c + 1) * P], prob[:, qt, c * P:(c + 1) * P])
                        mm.then_inc(prob_turned, 1)

                def apply_values(p, r, keys, k0, vh, vl, c0, pt_hi, pt_lo):
                    b = 2 + r % 2
                    pe.wait_ge(free[b], p[b] + r // 2)
                    for qt in range(2):
                        pe.wait_ge(free[6 + qt], p[6 + qt] + r + 1)
                    nk = keys // P
                    for c in range(nk):
                        t = k0 // P + c
                        mm = split_mm(ps[:, b, 0:256], vh[:, t, c0:c0 + P], vl[:, t, c0:c0 + P],
                                      pt_hi[:, c, :], pt_lo[:, c, :], c == 0, c == nk - 1)
                    mm.then_inc(av_done, 1)

                jobs = att_jobs(l, HEADS_C)
                p = PLAN["att_c", l]
                pe.wait_ge(bias_ready, 2 * l + 2)
                pe.wait_ge(free[0], p[0])
                pe.wait_ge(free[1], p[1])
                for r in range(-1, len(jobs) + 1):
                    if r + 1 < len(jobs):
                        h, q0, k0 = jobs[r + 1]
                        scores(p["att"] + r + 1, [(qc_hi[:, h], qc_lo[:, h], kc_hi[:, h], kc_lo[:, h], q0, k0)],
                               TOK - k0, h if q0 == 0 else None)
                    if 0 <= r < len(jobs):
                        turn_probs(p, r, TOK - jobs[r][2])
                    if r >= 1:
                        h, q0, k0 = jobs[r - 1]
                        apply_values(p, r - 1, TOK - k0, k0, vc_hi, vc_lo, h * P, ptc_hi, ptc_lo)

                p = PLAN["v_a", l]
                for k in range(KT):
                    wait_unit(p["unit"] + k)
                    if k == 0:
                        for tt in range(nt):
                            pe.wait_ge(free[tt], p[tt])
                    moving_unit(p["unit"] + k, h_hi, h_lo, k, nt, k == 0, k == KT - 1)
                p = PLAN["w_s", l]
                pe.wait_ge(gate_in, 48 * (l + 1))
                for g in range(4):
                    mm = turn(ps[:, 4, g * P:(g + 1) * P], ws_in[:, g, :])
                mm.then_inc(job_done, 1)
                ada(l, "v_a")
                for n in ("u", "g_a"):
                    tiles(n, l, nq)
                    ada(l, n)

                p = PLAN["mix_a", l]
                pe.wait_ge(op_ready, p["ready"])
                for g in range(4):
                    pe.wait_ge(free[2 + g % 2], p[2 + g % 2] + g // 2)
                    for tt in range(nt):
                        mm = pe.matmul(ps[:, 2 + g % 2, tt * P:(tt + 1) * P], z[:, VA + tt, g * P:(g + 1) * P],
                                       ws_t[:, g, :], start=True, stop=True)
                    mm.then_inc(job_done, 1)

                tiles("cq", l, nq)
                ada(l, "cq")
                tiles("ckv", l, TOK)
                ada(l, "ckv")

                p = PLAN["lat", l]
                pe.wait_ge(sq_sum, p["sq"])
                for c in range(nt + 4):
                    src = tmp[:, 2, c * P:(c + 1) * P] if c < nt else tmp[:, 3, (c - nt) * P:(c - nt + 1) * P]
                    mm = pe.matmul(ps[:, 4, c:c + 1], src, ones[:, 0:1], start=True, stop=True)
                mm.then_inc(job_done, 1)
                k = PLAN["kr", l]
                pe.wait_ge(free[2], k[2])
                for q in range(4):
                    wait_unit(k["unit"] + q)
                    stationary_unit(ps[:, 2, :], k["unit"] + q, h_hi, h_lo, 4 * q, TOK, q == 0, q == 3)
                pe.wait_ge(op_ready, p["ready"] + 1)
                pe.matmul(ps[:, 5, 0:nq], ones[:, :], tmp[:, 0, 0:nq], start=True, stop=True).then_inc(job_done, 1)
                pe.wait_ge(op_ready, p["ready"] + 2)
                pe.matmul(ps[:, 4, :], ones[:, :], tmp[:, 1, :], start=True, stop=True).then_inc(job_done, 1)
                pe.wait_ge(free[2], k[2] + 1)
                pe.wait_ge(free[3], k[3])
                pe.matmul(ps[:, 3, 0:SEQ], rot, prob[:, 0, 0:SEQ], start=True, stop=True).then_inc(job_done, 1)
                tiles("g_b", l, nq, 8)
                ada(l, "g_b")

                p = PLAN["v_b", l]
                pe.wait_ge(op_ready, p["ready"])
                for half in range(2):
                    for tt in range(4):
                        pe.wait_ge(free[tt], p[tt] + half)
                    for k in range(KL):
                        un = p["unit"] + 4 * half + k
                        wait_unit(un)
                        moving_unit(un, cv_hi, cv_lo, k, 4, k == 0, k == KL - 1)
                p = PLAN["q_r", l]
                for pair in range(5):
                    if pair < 4:
                        wait_unit(p["unit"] + pair)
                        pe.wait_ge(free[pair % 2], p[pair % 2] + pair // 2)
                        stationary_unit(ps[:, pair % 2, 0:nq], p["unit"] + pair, cq_hi, cq_lo, 0, nq, True, True)
                    if pair >= 1:
                        m = pair - 1
                        pe.wait_ge(free[m % 2], p[m % 2] + m // 2 + 1)
                        pe.wait_ge(free[2 + m % 2], p[2 + m % 2] + m // 2)
                        pe.matmul(ps[:, 2 + m % 2, 0:SEQ], rot, prob[:, m % 2, 0:SEQ], start=True, stop=True)\
                            .then_inc(job_done, 1)

                p = PLAN["heads", l]

                def head_operands(h):
                    for m, (bh, bl, n) in enumerate(((cq_hi, cq_lo, nq), (cv_hi, cv_lo, TOK))):
                        un = p["unit"] + 2 * h + m
                        wait_unit(un)
                        pe.wait_ge(free[m], p[m] + h)
                        stationary_unit(ps[:, m, 0:n], un, bh, bl, 0, n, True, True)

                jobs = att_jobs(l, HEADS_B)
                head_operands(0)
                pe.wait_ge(op_ready, p["ready"])
                for r in range(-1, len(jobs) + 1):
                    if r + 1 < len(jobs):
                        h, q0, k0 = jobs[r + 1]
                        if q0 == 0 and h + 1 < HEADS_B:
                            head_operands(h + 1)
                        if q0 == 0:
                            pe.wait_ge(free[0], p[0] + h + 1)
                            pe.wait_ge(free[1], p[1] + h + 1)
                        e = 2 * (h % 2)
                        scores(p["att"] + r + 1, [
                            (qk_hi[:, h % 2], qk_lo[:, h % 2], qk_hi[:, 2 + h % 2], qk_lo[:, 2 + h % 2], q0, k0),
                            (qr_hi[:, h // 2], qr_lo[:, h // 2], kr_ab[:, e], kr_ab[:, e + 1], q0, k0)], TOK - k0)
                    if 0 <= r < len(jobs):
                        turn_probs(p, r, TOK - jobs[r][2])
                    if r >= 1:
                        h, q0, k0 = jobs[r - 1]
                        apply_values(p, r - 1, TOK - k0, k0, v_hi, v_lo, h * P, ptb_hi, ptb_lo)

                p = PLAN["out", l]
                u = p["unit"]
                pe.wait_ge(free[0], p[0])
                for q in range(4):
                    wait_unit(u + q)
                    pe.wait_ge(op_ready, p["ready"] + 4 * q + 4)
                    stationary_unit(ps[:, 0, 0:nq], u + q, h_hi, h_lo, 4 * q, nq, q == 0, q == 3)
                pe.wait_ge(free[1], p[1])
                for q in range(4):
                    wait_unit(u + 4 + q)
                    stationary_unit(ps[:, 1, 0:nq], u + 4 + q, h_hi, h_lo, 4 * q, nq, q == 0, q == 3)
                for first, end in ((1, 3), (3, 5), (5, 7), (7, 8)) if l == 0 else ((1, 8),):
                    with pe.Fori(first, end) as i:
                        for j in range(2):
                            pe.wait_ge(free[j], p[j] + i)
                            for q in range(4):
                                wait_unit(u + 4 * j + q, i, 8)
                                stationary_unit(ps[:, j, 0:nq], u + 4 * j + q, h_hi, h_lo, 4 * q, nq, q == 0, q == 3)
                    if end < 8:
                        ada(l, f"out{first}")

            p = PLAN["end", 0]
            pe.wait_ge(free[1], p[1])
            for n in range(8):
                tt, g = n // 4, n % 4
                b = FINAL_BANKS[n]
                pe.wait_ge(free[b], p[b] + (1 if n >= 6 else 0))
                for c in range(4):
                    mm = turn(ps[:, b, c * P:(c + 1) * P], z[:, 4 * g + c, tt * P:(tt + 1) * P])
                mm.then_inc(job_done, 1)
                if n == 5:
                    pe.wait_ge(sq_sum, p["sq"])
                    for c in range(2):
                        mm = pe.matmul(ps[:, 4, c:c + 1], tmp[:, 2, c * P:(c + 1) * P], ones[:, 0:1],
                                       start=True, stop=True)
                    mm.then_inc(job_done, 1)

        @block.vector
        def _(dve):
            step, hi_n, t_n, sq_n, rdy_n = [0], [0], [0], [0], [0]

            def link(ins):
                step[0] += 1
                ins.then_inc(dve_step, 1)
                dve.wait_ge(dve_step, step[0])

            def prep(u, i=0, per=0):
                dve.wait_ge(hi_made, u + 1 + per * i)
                dst, src, top = w_lo[:, u % RING, :], w_raw[:, u % RAW, :], w_hi[:, u % RING, :]
                if per == 0 and u in KR_UNITS:
                    (dst, src), (top, _) = twice(dst, src), twice(top, src)
                dve.tensor_tensor(dst, src, top.bitcast(F32), ALU.subtract).then_inc(lo_made, 1)

            def prep_ahead(u, i=0, per=0):
                if u + AHEAD < UNITS:
                    prep(u + AHEAD, i, per)

            def next_hi():
                hi_n[0] += 1
                dve.wait_ge(op_hi, hi_n[0])

            def lo(dst, src, hi, scale=None):
                next_hi()
                if scale is None:
                    return dve.tensor_tensor(dst, src, hi.bitcast(F32), ALU.subtract)
                return dve.scalar_tensor_tensor(out=dst, in0=src, scalar=scale, in1=hi.bitcast(F32),
                                                op0=ALU.mult, op1=ALU.subtract)

            def rsqrt(n):
                v, r, t = small[:, 0:n], small[:, 10:10 + n], small[:, 20:20 + n]
                link(dve.tensor_single_scalar(t.bitcast(I32), v.bitcast(I32), 1, ALU.logical_shift_right))
                link(dve.tensor_scalar(r.bitcast(I32), t.bitcast(I32), -1.0, float(0x5F3759DF), ALU.mult, ALU.add))
                for _ in range(4):
                    link(dve.tensor_tensor(t, r, r, ALU.mult))
                    link(dve.tensor_tensor(t, t, v, ALU.mult))
                    link(dve.tensor_scalar(t, t, -0.5, 1.5, ALU.mult, ALU.add))
                    link(dve.tensor_tensor(r, r, t, ALU.mult))

            def mean_square(n, width, bank):
                link(dve.tensor_scalar(small[:, 0:n], ps[:, bank, 0:n], 1.0 / width, EPS, ALU.mult, ALU.add))

            def add_square(src, acc, n):
                sq_n[0] += 1
                dve.wait_ge(sq_ready, sq_n[0])
                dve.wait_ge(sq_sum, sq_n[0] - 1)
                dve.tensor_tensor(acc, acc, src, ALU.add).then_inc(sq_sum, 1)

            def ada_block(l, name):
                if (("ada", name), l) not in PLAN.at:
                    return None
                block = PLAN[("ada", name), l]["ada"]
                if block:
                    dve.wait_ge(ada_taken, block)
                for v in range(ada_vectors(block)):
                    dve.memset(ada_acc[:, v, :], 0.0).then_inc(ada_step, 1)
                return block

            def ada_add(block, s, i=0):
                if block is None:
                    return
                nv = ada_vectors(block)
                dve.wait_ge(ada_in[s % ADA_SLOTS], 16 * (4 * block + s // ADA_SLOTS + 1) + 32 * i)
                for v in range(nv):
                    dve.wait_ge(ada_step, ada_steps(block) + nv * s + v + 1 + 8 * nv * i)
                    dve.scalar_tensor_tensor(out=ada_acc[:, v, :], in0=ada_w[:, s % ADA_SLOTS, :],
                                             scalar=c_silu[:, bass.ds(v * KT + s + 8 * i, 1)],
                                             in1=ada_acc[:, v, :], op0=ALU.mult, op1=ALU.add).then_inc(ada_step, 1)

            def tiles(name, l, evac, count=4, start=0):
                u = PLAN[name, l]["unit"]
                block = ada_block(l, name)

                def turn(i, u, per, block=None):
                    for s in range(8):
                        if s == 4 and evac:
                            evac(i, 0)
                        prep_ahead(u + s, i, per)
                        ada_add(block, s, i - start)
                    if evac:
                        evac(i, 1)

                if name == "ckv":
                    turn(0, u, 0, block)
                    turn(1, u + 8, 0, block)
                    return
                with dve.Fori(start, start + 2) as i:
                    turn(i, u, 8, block)
                if start + 2 < count // 2:
                    with dve.Fori(start + 2, count // 2) as i:
                        turn(i, u, 8)

            def ada(l, after):
                if (("ada", after), l) not in PLAN.at:
                    return
                p = PLAN[("ada", after), l]
                c = 2 * KT + 4 * p["ada"]
                dve.wait_ge(ada_taken, p["ada"] + 1)
                nv = ada_vectors(p["ada"])
                for v in range(nv):
                    dve.tensor_reduce(mods[:, v, c:c + 4], ps[:, 6 + v, :].rearrange("p (c k) -> p c k", c=4),
                                      AX.X, ALU.add).then_inc(free[6 + v], 1)
                for v in range(nv):
                    dve.wait_ge(free[6 + v], p[6 + v] + 1)
                link(dve.tensor_tensor(mods[:, 0:nv, c:c + 4], mods[:, 0:nv, c:c + 4],
                                       cols[:, Q_BADA + c:Q_BADA + c + 4].unsqueeze(1).broadcast_to([P, nv, 4]), ALU.add))

            dve.wait_ge(job_done, 1)
            dve.tensor_copy(cols[:, 0:80], ps[:, 4, 0:80]).then_inc(free[4], 1)
            dve.wait_ge(job_done, 2)
            dve.tensor_copy(cols[:, 80:176], ps[:, 5, 0:96]).then_inc(free[5], 1)
            dve.wait_ge(op_hi, 2)
            for v in range(2):
                dve.tensor_tensor(c_st[:, :, 2 * v + 1], c_silu[:, v * KT:(v + 1) * KT],
                                  c_st[:, :, 2 * v].bitcast(F32), ALU.subtract).then_inc(op_ready, 1)
            hi_n[0] = 2
            link(dve.memset(tmp[:, 2, :], 0.0))
            for t in range(KT):
                add_square(tmp[:, t % 2, :], tmp[:, 2, :], TOK)

            for u in range(AHEAD):
                prep(u)
            j0 = PLAN["start", 0]["job"]
            with dve.Fori(0, START_BLOCKS) as b:
                for k in range(KT):
                    prep(k + AHEAD, b, KT)
                dve.wait_ge(job_done, j0 + 1 + b)
                dve.tensor_reduce(mods[:, :, bass.ds(4 * b, 4)].rearrange("p v c -> p c v"),
                                  ps[:, 2, 0:16].rearrange("p (c v k) -> p c v k", c=4, v=2), AX.X, ALU.add)\
                    .then_inc(free[2], 1)
            dve.wait_ge(free[2], START_BLOCKS)
            dve.wait_ge(free[5], 1)
            link(dve.tensor_tensor(mods[:, :, 0:32], mods[:, :, 0:32],
                                   cols[:, Q_BADA:Q_BADA + 32].unsqueeze(1).broadcast_to([P, 2, 32]), ALU.add))

            def nmax(j, keys):
                for qt in range(2):
                    n = 2 * j + qt
                    dve.wait_ge(scores_done, n + 1)
                    if n >= 2:
                        dve.wait_ge(exp_done, n - 1)
                    dve.tensor_reduce(small[:, 40 + qt:41 + qt], ps[:, 4 + qt, 0:keys], AX.X, ALU.max, negate=True)\
                        .then_inc(nmax_ready, 1)

            def normalise(j, keys):
                for qt in range(2):
                    dve.wait_ge(exp_done, 2 * j + qt + 1)
                    link(dve.reciprocal(small[:, 44 + qt:45 + qt], small[:, 42 + qt:43 + qt]))
                    dve.tensor_scalar(prob[:, qt, 0:keys], prob[:, qt, 0:keys], small[:, 44 + qt:45 + qt], None,
                                      ALU.mult).then_inc(prob_ready, 1)

            def turned_lo(keys, pt_hi, pt_lo):
                nk = keys // P
                for qt in range(2):
                    q = slice(qt * P, (qt + 1) * P)
                    lo(pt_lo[:, 0:nk, q], ps[:, 6 + qt, 0:keys].rearrange("p (k q) -> p k q", k=nk),
                       pt_hi[:, 0:nk, q]).then_inc(free[6 + qt], 1)

            def mix(j, r, tile, q0):
                dve.wait_ge(av_done, j + 1)
                dve.tensor_tensor(z[:, tile, q0:q0 + SEQ], ps[:, 2 + r % 2, 0:SEQ], z[:, tile, q0:q0 + SEQ], ALU.mult)\
                    .then_inc(free[2 + r % 2], 1)

            for l in range(DEPTH):
                nt = query_tiles(l)
                nq = nt * P
                link(dve.scalar_tensor_tensor(out=a_col[:, :, :], in0=mods[:, :, 48 * l + KT:48 * l + 2 * KT], scalar=1.0,
                                              in1=cols[:, Q_NG + KT * l:Q_NG + KT * (l + 1)].unsqueeze(1)
                                              .broadcast_to([P, 2, KT]), op0=ALU.add, op1=ALU.mult))
                p = PLAN["head", l]
                dve.wait_ge(job_done, p["job"] + 1)
                mean_square(4, D, 4)
                rsqrt(4)
                for c in range(4):
                    ins = dve.tensor_scalar(tmp[:, 3, c * P:(c + 1) * P], ident, small[:, 10 + c:11 + c], None, ALU.mult)
                ins.then_inc(op_ready, 1)
                dve.wait_ge(job_done, p["job"] + 2)
                u = PLAN["v_c", l]["unit"]

                def scaled(k):
                    if k >= 2:
                        dve.wait_ge(op_ready, p["ready"] + k)
                    for v in range(2):
                        t = slice(v * SEQ, (v + 1) * SEQ)
                        ins = dve.scalar_tensor_tensor(out=tmp[:, k % 2, t], in0=z[:, k, t], scalar=a_col[:, v, k:k + 1],
                                                       in1=ps[:, 5, t], op0=ALU.mult, op1=ALU.mult)
                    ins.then_inc(t_ready, 1)

                scaled(0)
                t0 = t_n[0]
                for k in range(KT):
                    if k + 1 < KT:
                        scaled(k + 1)
                    next_hi()
                    dve.wait_ge(t_ready, t0 + k + 1)
                    for v in range(2):
                        t = slice(v * SEQ, (v + 1) * SEQ)
                        ins = dve.scalar_tensor_tensor(out=h_lo[:, k, t], in0=tmp[:, k % 2, t],
                                                       scalar=mods[:, v, 48 * l + k:48 * l + k + 1],
                                                       in1=h_hi[:, k, t].bitcast(F32), op0=ALU.add, op1=ALU.subtract)
                    ins.then_inc(op_ready, 1)
                    if k >= 2:
                        prep_ahead(u + k - 2)
                t_n[0] += KT
                prep_ahead(u + KT - 2)
                prep_ahead(u + KT - 1)
                for tt in range(4):
                    lo(vc_lo[:, tt, :], ps[:, tt, :], vc_hi[:, tt, :]).then_inc(free[tt], 1)

                def split_tile(dst_lo, dst_hi, n, scale, h0):
                    def evac(i, j):
                        dve.wait_ge(op_hi, h0 + 1 + j + 2 * i)
                        t = bass.ds(2 * i + j, 1)
                        dve.scalar_tensor_tensor(out=dst_lo[:, t, 0:n], in0=ps[:, j:j + 1, 0:n], scalar=scale,
                                                 in1=dst_hi[:, t, 0:n].bitcast(F32), op0=ALU.mult, op1=ALU.subtract)\
                            .then_inc(free[j], 1)
                    return evac

                tiles("q_c", l, split_tile(qc_lo, qc_hi, nq, C_SCALE, hi_n[0]))
                hi_n[0] += 4
                ada(l, "q_c")
                tiles("k_c", l, split_tile(kc_lo, kc_hi, TOK, 1.0, hi_n[0]))
                hi_n[0] += 4
                ada(l, "k_c")
                tiles("g_c", l, None)
                ada(l, "g_c")

                def attention(name, heads, tile0, pt_hi, pt_lo, operands):
                    jobs = att_jobs(l, heads)
                    p = PLAN[name, l]
                    for r in range(-1, len(jobs) + 1):
                        if r + 1 < len(jobs):
                            h, q0, k0 = jobs[r + 1]
                            if operands and q0 == 0 and h + 1 < heads:
                                operands(h + 1)
                            j = p["att"] + r + 1
                            nmax(j, TOK - k0)
                            normalise(j, TOK - k0)
                        if 0 <= r < len(jobs):
                            turned_lo(TOK - jobs[r][2], pt_hi, pt_lo)
                        if r >= 1:
                            h, q0, k0 = jobs[r - 1]
                            mix(p["att"] + r - 1, r - 1, tile0 + h, q0)

                dve.wait_ge(free[1], PLAN["att_c", l][1])
                dve.wait_ge(free[0], PLAN["att_c", l][0])
                attention("att_c", HEADS_C, 12, ptc_hi, ptc_lo, None)

                p = PLAN["v_a", l]
                block = ada_block(l, "v_a")
                for k in range(KT):
                    prep_ahead(p["unit"] + k)
                    ada_add(block, k)
                dve.wait_ge(gate_in, 48 * (l + 1))
                for tt in range(nt):
                    dve.wait_ge(free[tt], p[tt] + 1)
                    ins = dve.tensor_tensor_reduce(tmp[:, 0, :], z[:, VA + tt, :], z[:, VA + tt, :], 1.0, 0.0,
                                                   ALU.mult, ALU.add, small[:, 30 + tt:31 + tt])
                    link(ins)
                link(dve.tensor_scalar(small[:, 0:nt], small[:, 30:30 + nt], 1.0 / W_A, EPS, ALU.mult, ALU.add))
                rsqrt(nt)
                for tt in range(nt):
                    ins = dve.scalar_tensor_tensor(out=z[:, VA + tt, :], in0=z[:, VA + tt, :],
                                                   scalar=small[:, 10 + tt:11 + tt], in1=sgu_row[:, :],
                                                   op0=ALU.mult, op1=ALU.mult)
                ins.then_inc(op_ready, 1)
                p = PLAN["w_s", l]
                dve.wait_ge(job_done, p["job"] + 1)
                dve.tensor_copy(ws_t[:, :, :].rearrange("p g q -> p (g q)"), ps[:, 4, :]).then_inc(op_ready, 1)
                ada(l, "v_a")
                tiles("u", l, None)
                ada(l, "u")
                tiles("g_a", l, None)
                ada(l, "g_a")

                p = PLAN["mix_a", l]
                dve.wait_ge(op_ready, p["ready"])
                dve.wait_ge(free[0], p[0])
                dve.wait_ge(free[1], p[1])
                for g in range(4):
                    link(dve.tensor_tensor(z[:, g, 0:nq], z[:, g, 0:nq], z[:, UG + g, 0:nq], ALU.mult))
                    dve.wait_ge(job_done, p["job"] + g + 1)
                    dve.tensor_tensor(tmp[:, g % 2, 0:nq].rearrange("p (t q) -> p t q", t=nt),
                                      ps[:, 2 + g % 2, 0:nq].rearrange("p (t q) -> p t q", t=nt),
                                      bs_row[:, g, :].unsqueeze(1).broadcast_to([P, nt, P]), ALU.add)\
                        .then_inc(free[2 + g % 2], 1)
                    dve.wait_ge(free[2 + g % 2], p[2 + g % 2] + g // 2 + 1)
                    ins = dve.tensor_tensor(z[:, g, 0:nq], z[:, g, 0:nq], tmp[:, g % 2, 0:nq], ALU.mult)
                ins.then_inc(op_ready, 1)
                for a in range(2):
                    link(dve.memset(tmp[:, 2 + a, :], 0.0))

                def latent_square(acc, n):
                    sq0 = sq_n[0]
                    def evac(i, j):
                        dve.wait_ge(sq_ready, sq0 + 1 + j + 2 * i)
                        dve.wait_ge(sq_sum, sq0 + j + 2 * i)
                        dve.tensor_tensor(tmp[:, acc, 0:n], tmp[:, acc, 0:n], tmp[:, j, 0:n], ALU.add)\
                            .then_inc(sq_sum, 1)
                    return evac

                tiles("cq", l, latent_square(2, nq))
                sq_n[0] += 4
                ada(l, "cq")
                tiles("ckv", l, latent_square(3, TOK))
                sq_n[0] += 4
                ada(l, "ckv")

                p = PLAN["lat", l]
                dve.wait_ge(job_done, p["job"] + 1)
                mean_square(nt + 4, LORA, 4)
                rsqrt(nt + 4)
                for a, (c0, n) in enumerate(((0, nt), (nt, 4))):
                    for c in range(n):
                        ins = dve.tensor_scalar(tmp[:, a, c * P:(c + 1) * P], ident, small[:, 10 + c0 + c:11 + c0 + c],
                                                None, ALU.mult)
                    ins.then_inc(op_ready, 1)
                for q in range(4):
                    prep_ahead(PLAN["kr", l]["unit"] + q)

                u = PLAN["g_b", l]["unit"]

                def latent_normed(s):
                    n = nq if s < KL else TOK
                    if s in (0, KL):
                        dve.wait_ge(job_done, p["job"] + (2 if s == 0 else 3))
                    if s >= 2:
                        dve.wait_ge(op_ready, PLAN["latn", l]["ready"] + s - 1)
                    g = (Q_QA if s < KL else Q_KV) + KL * l + s % KL
                    dve.scalar_tensor_tensor(out=tmp[:, 2 + s % 2, 0:n], in0=z[:, RAWL + s, 0:n],
                                             scalar=cols[:, g:g + 1],
                                             in1=ps[:, 5 if s < KL else 4, 0:n], op0=ALU.mult, op1=ALU.mult)\
                        .then_inc(t_ready, 1)

                latent_normed(0)
                t0 = t_n[0]
                for s in range(8):
                    if s + 1 < 8:
                        latent_normed(s + 1)
                    n = nq if s < KL else TOK
                    dh, dl = (cq_hi, cq_lo) if s < KL else (cv_hi, cv_lo)
                    dve.wait_ge(t_ready, t0 + s + 1)
                    lo(dl[:, s % KL, 0:n], tmp[:, 2 + s % 2, 0:n], dh[:, s % KL, 0:n]).then_inc(op_ready, 1)
                    prep_ahead(u + s)
                t_n[0] += 8
                k = PLAN["kr", l]
                dve.wait_ge(job_done, k["job"] + 1)
                dve.memset(kr_ab[ROPE:P, 0:2, :].bitcast(F32), 0.0)
                dve.memset(kr_ab[0:ROPE, 2:4, :].bitcast(F32), 0.0)
                dve.tensor_tensor(prob[:, 1, 0:SEQ], prob[:, 0, 0:SEQ], cos, ALU.mult)
                dve.tensor_tensor(prob[:, 1, SEQ:TOK], ps[:, 3, 0:SEQ], sin, ALU.mult).then_inc(free[3], 1)
                dve.wait_ge(free[3], k[3] + 1)
                dve.tensor_tensor(prob[:, 0, 0:SEQ], prob[:, 1, 0:SEQ], prob[:, 1, SEQ:TOK], ALU.add).then_inc(t_ready, 1)
                t_n[0] += 1
                dve.wait_ge(t_ready, t_n[0])
                lo(kr_ab[0:ROPE, 1, :], prob[0:ROPE, 0, :], kr_ab[0:ROPE, 0, :]).then_inc(op_ready, 1)
                lo(kr_ab[ROPE:P, 3, :], prob[ROPE:P, 0, :], kr_ab[ROPE:P, 2, :]).then_inc(op_ready, 1)
                tiles("g_b", l, None, 8, 1)
                ada(l, "g_b")

                u = PLAN["v_b", l]["unit"]
                for half in range(2):
                    for k in range(KL):
                        prep_ahead(u + 4 * half + k)
                    for tt in range(4):
                        c = slice(half * 512, half * 512 + 512)
                        lo(v_lo[:, tt, c], ps[:, tt, :], v_hi[:, tt, c]).then_inc(free[tt], 1)

                p = PLAN["q_r", l]
                for pair in range(5):
                    if pair < 4:
                        prep_ahead(p["unit"] + pair)
                    if pair >= 1:
                        m = pair - 1
                        dve.wait_ge(job_done, p["job"] + m + 1)
                        dst = tmp[:, 2 + m % 2, :]
                        dve.scalar_tensor_tensor(out=tmp[:, 0, 0:SEQ], in0=prob[:, m % 2, 0:SEQ], scalar=MLA_SCALE,
                                                 in1=cos, op0=ALU.mult, op1=ALU.mult)
                        dve.scalar_tensor_tensor(out=tmp[:, 1, 0:SEQ], in0=ps[:, 2 + m % 2, 0:SEQ], scalar=MLA_SCALE,
                                                 in1=sin, op0=ALU.mult, op1=ALU.mult).then_inc(free[2 + m % 2], 1)
                        dve.wait_ge(free[2 + m % 2], p[2 + m % 2] + m // 2 + 1)
                        if nq > SEQ:
                            dve.tensor_scalar(dst[:, SEQ:TOK], prob[:, m % 2, SEQ:TOK], MLA_SCALE, None, ALU.mult)
                        dve.tensor_tensor(dst[:, 0:SEQ], tmp[:, 0, 0:SEQ], tmp[:, 1, 0:SEQ], ALU.add).then_inc(t_ready, 1)
                        t_n[0] += 1
                        dve.wait_ge(t_ready, t_n[0])
                        lo(qr_lo[:, m, 0:nq], dst[:, 0:nq], qr_hi[:, m, 0:nq]).then_inc(op_ready, 1)

                p = PLAN["heads", l]

                def head_operands(h):
                    prep_ahead(p["unit"] + 2 * h)
                    lo(qk_lo[:, h % 2, 0:nq], ps[:, 0, 0:nq], qk_hi[:, h % 2, 0:nq], MLA_SCALE).then_inc(free[0], 1)
                    prep_ahead(p["unit"] + 2 * h + 1)
                    lo(qk_lo[:, 2 + h % 2, :], ps[:, 1, :], qk_hi[:, 2 + h % 2, :]).then_inc(free[1], 1)

                head_operands(0)
                attention("heads", HEADS_B, 4, ptb_hi, ptb_lo, head_operands)

                p = PLAN["out", l]
                u = p["unit"]
                link(dve.memset(tmp[:, 2, :], 0.0))
                gate = 48 * l + 2 * KT

                def new_x(i, j):
                    dve.wait_ge(unit_done, u + 4 * (j + 1) + 8 * i)
                    dve.wait_ge(x_back[j], 16 * (KT // 2) * l + 16 * (i + 1))
                    t = bass.ds(2 * i + j, 1)
                    for v in range(nq // SEQ):
                        c = slice(v * SEQ, (v + 1) * SEQ)
                        ins = dve.scalar_tensor_tensor(out=z[:, t, c], in0=ps[:, j:j + 1, c],
                                                       scalar=mods[:, v, bass.ds(gate + 2 * i + j, 1)],
                                                       in1=x_res[:, j:j + 1, c], op0=ALU.mult, op1=ALU.add)
                    ins.then_inc(free[j], 1)

                sq0 = sq_n[0]

                def square(i, j):
                    dve.wait_ge(sq_ready, sq0 + 1 + j + 2 * i)
                    dve.wait_ge(sq_sum, sq0 + j + 2 * i)
                    dve.tensor_tensor(tmp[:, 2, 0:nq], tmp[:, 2, 0:nq], tmp[:, j, 0:nq], ALU.add).then_inc(sq_sum, 1)

                for t in range(KT):
                    lo(h_lo[:, t, 0:nq], z[:, t, 0:nq], h_hi[:, t, 0:nq]).then_inc(op_ready, 1)
                    if t % 4 == 3:
                        prep_ahead(u + t // 4)
                new_x(0, 0)
                for s in range(4, 8):
                    prep_ahead(u + s)
                square(0, 0)
                new_x(0, 1)

                def turn_pair(i, u8, per, block=None, start=0):
                    for s in range(8):
                        if s == 4:
                            square(i - 1, 1)
                            new_x(i, 0)
                        prep_ahead(u8 + s, i if per else 0, per)
                        ada_add(block, s, i - start)
                    square(i, 0)
                    new_x(i, 1)

                if l == 0:
                    for first in (1, 3, 5):
                        block = ada_block(l, f"out{first}")
                        with dve.Fori(first, first + 2) as i:
                            turn_pair(i, u, 8, block, first)
                        ada(l, f"out{first}")
                    turn_pair(KT // 2 - 1, u + 8 * (KT // 2 - 1), 0)
                else:
                    with dve.Fori(1, KT // 2 - 1) as i:
                        turn_pair(i, u, 8)
                    turn_pair(KT // 2 - 1, u + 8 * (KT // 2 - 1), 0)
                square(KT // 2 - 1, 1)
                sq_n[0] += KT

            p = PLAN["end", 0]
            dve.wait_ge(fg_in, 16)
            dve.wait_ge(job_done, p["job"] + 7)
            mean_square(2, D, 4)
            rsqrt(2)
            for n in range(8):
                tt, g = n // 4, n % 4
                b = FINAL_BANKS[n]
                dve.wait_ge(job_done, p["job"] + (n + 1 if n < 6 else n + 2))
                c = slice(g * 512, (g + 1) * 512)
                ins = dve.scalar_tensor_tensor(out=y[:, tt, c], in0=ps[:, b, :], scalar=small[:, 10 + tt:11 + tt],
                                               in1=fg_row[:, c], op0=ALU.mult, op1=ALU.mult)
                ins.then_inc(free[b], 1)


def constants():
    f = np.float32
    c = np.zeros((P, C_N), f)
    c[:, C_ID:C_ID + P] = np.eye(P, dtype=f)
    q = ROPE // 4
    for m in range(P):
        b = m % (2 * q)
        if b < q:
            c[m + q, C_ROT + m] = -1.0
        else:
            c[m - q, C_ROT + m] = 1.0
    t = np.arange(SEQ)
    inv = f(10000.0) ** (-np.arange(q, dtype=f) / f(q))
    pos = np.stack([(t // GRID_W).astype(f), (t % GRID_W).astype(f)])
    for m in range(P):
        ang = (pos[(m % ROPE) // (2 * q)] * inv[m % q]).astype(f)
        c[m, C_COS:C_COS + SEQ] = np.cos(ang)
        c[m, C_SIN:C_SIN + SEQ] = np.sin(ang)
    col = np.arange(GRID_W)
    c0 = np.clip(col - 8, 0, GRID_W - 16)
    ok = (col[None, :] >= c0[:, None]) & (col[None, :] < c0[:, None] + 16)
    ok = np.concatenate([ok, ok])
    ok = ok[::-1]
    c[:, C_TURN:C_TURN + P] = np.kron(np.eye(2), np.eye(GRID_W)[::-1]).astype(f)
    c[:, C_KEEP:C_KEEP + GRID_W] = ok
    c[:, C_MASK:C_MASK + GRID_W] = np.where(ok, f(0), f(NEG))
    return c


def kernel(**inputs):
    import concourse.bacc as bacc
    from concourse.bass_utils import run_bass_kernel_spmd

    a = {n: np.ascontiguousarray(v) for n, v in inputs.items()}
    rows = {
        "rows_a": np.concatenate([a["c"].reshape(KT, P), a["c_ctx"].reshape(KT, P), a["norm_g"].reshape(-1, P),
                                  a["qa_g"].reshape(-1, P), a["kva_g"].reshape(-1, P)]),
        "rows_b": a["b_ada"].reshape(-1, P),
        "consts": constants(),
    }
    nc = bacc.Bacc("TRN2", target_bir_lowering=False, num_devices=1)
    arrays, args = {}, []
    names = ["x", "ctx", "w_ada", "w_in", "w_uq", "w_ukv", "sgu_g", "w_s", "b_s", "rpb", "w_out", "final_g"]
    for n in names + list(rows):
        v = np.ascontiguousarray(a[n] if n in names else rows[n])
        arrays[f"in_{n}"] = v
        args.append(nc.dram_tensor(f"in_{n}", v.shape, mybir.dt.from_np(v.dtype), kind="ExternalInput").ap())
    args.append(nc.dram_tensor("out_x", (1, SEQ, D), F32, kind="ExternalOutput").ap())
    hybrid_kernel(nc, *args)
    r = run_bass_kernel_spmd(nc, [arrays], core_ids=[0])
    return r.results[0]["out_x"]
```

```python
from contextlib import ExitStack

import numpy as np

import concourse.bass as bass
from concourse import mybir

F32 = mybir.dt.float32
R32 = mybir.dt.float32r
I32 = mybir.dt.int32
ALU = mybir.AluOpType
ACT = mybir.ActivationFunctionType
AX = mybir.AxisListType

P = 128
D = 2048
KT = D // P
SEQ = CTX = 256
TOK = SEQ + CTX
DEPTH = 2
W_A, W_B, W_C = D // 4, D // 2, D // 4
HEADS_A, HEADS_B, HEADS_C = W_A // P, W_B // P, W_C // P
LORA = 512
KL = LORA // P
NOPE, ROPE = 128, 64
GRID_W = 64
ROWS = SEQ // GRID_W
IN_W = 3 * W_A + 2 * LORA + ROPE + W_B + 4 * W_C
EPS = 1e-6
MLA_SCALE = float((NOPE + ROPE) ** -0.5)
C_SCALE = float(P ** -0.5)
RPB_H, RPB_W = 15, 31
NEG = -1e30

COL = {}
_at = 0
for _n, _w in (("u", W_A), ("v_a", W_A), ("g_a", W_A), ("cq", LORA), ("ckv", LORA), ("kr", ROPE),
               ("g_b", W_B), ("q_c", W_C), ("k_c", W_C), ("v_c", W_C), ("g_c", W_C)):
    COL[_n] = _at
    _at += _w
assert _at == IN_W

RAW, RING, AHEAD = 8, 4, 3
FINAL_BANKS = (6, 7, 0, 1, 2, 3, 6, 7)
GROUPS = D // 512
CHUNK_AT = (4, 11, 18, 25)
OUT_TILES = (*range(0, 4), *range(12, 16), *range(4, 12))
OUT_FIRST = ((0, 0), (1, 0), (0, 1), (1, 1), (0, 2), (0, 3), (1, 2), (1, 3))
V_C_BANK = (4, 0)
ADA_BLOCKS = 16
ADA_SLOTS = 4
ADA_BOTH = 12

C_ID, C_ROT, C_COS, C_SIN, C_TURN, C_KEEP, C_MASK, C_N = 0, 128, 256, 512, 768, 896, 960, 1024
Q_C, Q_NG, Q_QA, Q_KV, Q_FG, Q_BADA, Q_N = 0, 32, 64, 72, 80, 96, 192


def query_tiles(l):
    return 4 if l < DEPTH - 1 else 2


def early_tiles(l, r):
    jobs = att_jobs(l, HEADS_B)
    start = jobs.index((HEADS_B - 2, 0, 0)) - 1
    n = 8 // (len(jobs) - 1 - start)
    return [n * (r - start) + i for i in range(n)] if start <= r < len(jobs) - 1 else []


def att_jobs(l, heads):
    out = []
    for h in range(heads):
        out.append((h, 0, 0))
        if l < DEPTH - 1:
            out.append((h, SEQ, SEQ))
    return out


def ada_bank(l, name):
    return 2 if (l, name) == (0, "v_c") else 6


def ada_vectors(block):
    return 2 if block < ADA_BOTH else 1


class Plan:

    def __init__(self):
        self.at = {}
        self.now = {"unit": 0, "job": 0, "ready": 0, "sq": 0, "att": 0, "ada": 0, **{b: 0 for b in range(8)}}
        add = self.add
        add("cols", 0, job=2, b={4: 1, 5: 1}, ready=2)
        add("start", 0, unit=2 * KT * GROUPS, job=1, sq=2, ready=KT,
            b={**{j: KT // 4 + 1 for j in range(4)}, 4: GROUPS, 6: GROUPS, 5: 2 * GROUPS, 7: 1})
        for l in range(DEPTH):
            nt = query_tiles(l)
            jobs_c, jobs_b = len(att_jobs(l, HEADS_C)), len(att_jobs(l, HEADS_B))
            if l:
                add("head", l, job=2, ready=1 + KT)
            add("v_c", l, unit=KT, b={V_C_BANK[l] + tt: 1 for tt in range(4)})
            self.ada(l, "v_c")
            for n in ("k_c", "g_c") if l == 0 else ("q_c", "k_c", "g_c"):
                add(n, l, unit=16, b={0: 2, 1: 2})
                if n != "g_c":
                    self.ada(l, n)
            add("att_c", l, att=jobs_c, b={6: jobs_c, 7: jobs_c, 2: (jobs_c + 1) // 2, 3: jobs_c // 2})
            self.ada(l, "g_c")
            add("v_a", l, unit=KT, b={i: 1 for i in range(nt)}, ready=1)
            add("w_s", l, job=1, ready=1)
            self.ada(l, "v_a")
            for n in ("u", "g_a"):
                add(n, l, unit=16, b={0: 2, 1: 2})
                self.ada(l, n)
            add("mix_a", l, job=4, b={2: 1, 3: 1, 4: 1, 5: 1}, ready=1)
            for n in ("cq", "ckv"):
                add(n, l, unit=16, b={0: 2, 1: 2}, sq=4)
                self.ada(l, n)
            add("lat", l, job=3, ready=2)
            add("kr", l, unit=4, job=1, b={2: 1, 3: 1})
            add("latn", l, ready=2 * KL)
            add("krn", l, ready=2)
            add("g_b", l, unit=32, b={0: 4, 1: 4})
            add("v_b", l, unit=8, b={i: 1 for i in range(4)})
            self.ada(l, "g_b")
            add("v_b2", l, b={i: 1 for i in range(4, 8)})
            add("q_r", l, unit=4, job=4, b={0: 2, 1: 2, 2: 2, 3: 2}, ready=4)
            add("heads", l, unit=2 * HEADS_B, att=jobs_b,
                b={0: HEADS_B, 1: HEADS_B, 6: jobs_b, 7: jobs_b,
                   2: (jobs_b + 1) // 2, 3: jobs_b // 2})
            for n in ("out1", "out3", "out5"):
                self.ada(l, n)
            add("out", l, unit=64, ready=KT, b={0: 8, 1: 8}, sq=KT)
        add("end", 0)
        assert self.now["ada"] == ADA_BLOCKS

    def add(self, name, l, b=None, **more):
        self.at[name, l] = dict(self.now)
        for k, v in {**(b or {}), **more}.items():
            self.now[k] += v

    ADA_IN = {0: ("v_c", "k_c", "g_c", "v_a", "u", "g_a", "cq", "ckv", "g_b", "out1", "out3", "out5"),
              1: ("k_c", "g_c", "ckv", "g_b")}

    def ada(self, l, after):
        if after in self.ADA_IN[l]:
            b = ada_bank(l, after)
            self.add(("ada", after), l, b={b: 1, b + 1: ada_vectors(self.now["ada"]) - 1}, ada=1)

    def __getitem__(self, key):
        return self.at[key]


PLAN = Plan()


def ada_steps(block):
    return (KT + 1) * (2 * min(block, ADA_BOTH) + max(0, block - ADA_BOTH))
UNITS = PLAN["end", 0]["unit"]


KR_UNITS = [PLAN["kr", l]["unit"] + q for l in range(DEPTH) for q in range(4)]


def twice(dst, src):
    return (dst.rearrange("p (k t n) -> p k t n", k=4, t=2),
            src.rearrange("p (k n) -> p k n", k=4)[:, :, 0:ROPE].unsqueeze(2).broadcast_to([P, 4, 2, ROPE]))


def raw_extra(u):
    two = [PLAN["q_r", l]["unit"] + i for l in range(DEPTH) for i in range(4)]
    return 16 * sum(1 for t in two if t <= u and t % RAW == u % RAW)


def hybrid_kernel(nc, x, ctx_in, w_ada, w_in, w_uq, w_ukv, sgu_g, w_s, b_s, rpb, w_out,
                  rows_a, rows_b, consts, out):
    x_scratch = nc.dram_tensor("x_scratch", (P, KT, TOK), F32).ap()

    with ExitStack() as stack:
        def sem(name):
            return stack.enter_context(nc.semaphore(name))

        stack.enter_context(nc.sbuf_tensor("arena", [P, 207 * 256], F32))
        base = (16481 + 31) // 32 * 32

        def at(name, kib, shape, dt=F32):
            return nc.alloc_sbuf_tensor_at(name, [P, *shape], dt, offset=base + int(kib * 1024))

        h_hi, h_lo = at("h_hi", 0, [KT, TOK], R32), at("h_lo", 32, [KT, TOK], R32)
        c_st = at("c_st", 128, [KT, P], R32)
        xn, junk = at("xn", 96, [4, TOK]), at("junk", 104, [D])
        q_whi, q_wlo = at("q_whi", 112, [2, 512], R32), at("q_wlo", 116, [2, 512], R32)
        x_in = at("x_in", 32, [4, D])
        v_hi, v_lo = at("v_hi", 0, [4, W_B], R32), at("v_lo", 32, [4, W_B], R32)
        qr_hi, qr_lo = at("qr_hi", 16, [4, TOK], R32), at("qr_lo", 48, [4, TOK], R32)
        qk_hi, qk_lo = at("qk_hi", 24, [4, TOK], R32), at("qk_lo", 56, [4, TOK], R32)
        z = at("z", 64, [KT, TOK])
        kc_hi, kc_lo = at("kc_hi", 64, [4, TOK], R32), at("kc_lo", 72, [4, TOK], R32)
        VA, UG, RAWL = 4, 8, 4
        vc_hi, vc_lo = at("vc_hi", 96, [4, W_C], R32), at("vc_lo", 104, [4, W_C], R32)
        qc_hi, qc_lo = at("qc_hi", 112, [4, TOK], R32), at("qc_lo", 120, [4, TOK], R32)
        cv_hi, cv_lo = at("cv_hi", 96, [KL, TOK], R32), at("cv_lo", 104, [KL, TOK], R32)
        cq_hi, cq_lo = at("cq_hi", 112, [KL, TOK], R32), at("cq_lo", 120, [KL, TOK], R32)
        oa_hi, oa_lo = at("oa_hi", 96, [8, TOK], R32), at("oa_lo", 112, [8, TOK], R32)
        ob_hi, ob_lo = at("ob_hi", 16, [8, TOK], R32), at("ob_lo", 48, [8, TOK], R32)
        kr_ab = at("kr_ab", 128, [4, TOK], R32)
        ptc_hi, ptc_lo = at("ptc_hi", 128, [4, 256], R32), at("ptc_lo", 132, [4, 256], R32)
        y = at("y", 32, [2, D])
        xg = at("xg", 0, [KT, SEQ])
        w_raw = at("w_raw", 136, [RAW, 512])
        w_hi, w_lo = at("w_hi", 152, [RING, 512], R32), at("w_lo", 160, [RING, 512], R32)
        ada_w = at("ada_w", 168, [ADA_SLOTS, 512])
        ada_acc = at("ada_acc", 176, [2, 512])
        bias = at("bias", 180, [8, 256])
        bs_row, sgu_row = at("bs_row", 180, [4, P]), at("sgu_row", 182, [W_A])
        ws_t, ws_in = at("ws_t", 184, [4, P]), at("ws_in", 186, [4, P])
        ptb_hi, ptb_lo = at("ptb_hi", 180, [4, 256], R32), at("ptb_lo", 184, [4, 256], R32)
        x_res = at("x_res", 180, [2, TOK])
        prob = at("prob", 188, [2, TOK])
        tmp = at("tmp", 192, [4, TOK])
        cst = at("cst", 200, [C_N])
        ones = at("ones", 204.0, [P])
        cols = at("cols", 204.5, [Q_N])
        mods = at("mods", 205.25, [2, 96])
        c_silu = at("c_silu", 206.0, [32])
        a_col = at("a_col", 206.125, [2, KT])
        small = at("small", 206.25, [60])
        ident, rot = cst[:, C_ID:C_ID + P], cst[:, C_ROT:C_ROT + P]
        turn_rows = cst[:, C_TURN:C_TURN + P]
        cos, sin = cst[:, C_COS:C_COS + SEQ], cst[:, C_SIN:C_SIN + SEQ]

        ps = stack.enter_context(nc.psum_tensor("ps", [P, 8, 512], F32))

        raw_in = [sem(f"raw_in{i}") for i in range(RAW)]
        hi_made, lo_made = sem("hi_made"), sem("lo_made")
        unit_done = sem("unit_done")
        free = [sem(f"free{b}") for b in range(8)]
        job_done = sem("job_done")
        op_hi = sem("op_hi")
        op_ready = sem("op_ready")
        t_ready = sem("t_ready")
        sq_ready, sq_sum = sem("sq_ready"), sem("sq_sum")
        scores_done, nmax_ready, exp_done = sem("scores_done"), sem("nmax_ready"), sem("exp_done")
        prob_ready, prob_turned, av_done = sem("prob_ready"), sem("prob_turned"), sem("av_done")
        dve_step, act_step = sem("dve_step"), sem("act_step")
        rows_in, const_in = sem("rows_in"), sem("const_in")
        x_landed = [sem(f"x_landed{tt}") for tt in range(4)]
        x_turned, rows_turned = sem("x_turned"), sem("rows_turned")
        mod_step, group_ready = sem("mod_step"), sem("group_ready")
        xn_ready = sem("xn_ready")
        q_hi_made, q_lo_made, q_done = sem("q_hi_made"), sem("q_lo_made"), sem("q_done")
        bias_in, gate_in, xg_ready = sem("bias_in"), sem("gate_in"), sem("xg_ready")
        bias_ready, pool_set = sem("bias_ready"), sem("pool_set")
        ada_in = [sem(f"ada_in{i}") for i in range(ADA_SLOTS)]
        ada_step = sem("ada_step")
        ada_taken = sem("ada_taken")
        x_kept, x_back = sem("x_kept"), [sem("x_back0"), sem("x_back1")]
        out_stored, final_rms = sem("out_stored"), sem("final_rms")

        block = stack.enter_context(nc.Block())

        @block.sync
        def _(sp):
            sp.dma_start(tmp[0:Q_BADA, 0, 0:P], rows_a).then_inc(rows_in, 16)
            sp.dma_start(tmp[0:Q_N - Q_BADA, 1, 0:P], rows_b).then_inc(rows_in, 16)
            sp.dma_start(cst[:, :], consts).then_inc(const_in, 16)
            for tt in range(4):
                src = (x if tt < 2 else ctx_in)[0, (tt % 2) * P:(tt % 2 + 1) * P, :]
                sp.dma_start(x_in[:, tt, :], src).then_inc(x_landed[tt], 16)

            def slot_free(u, i=0, per=0):
                if u >= RAW:
                    sp.wait_ge(lo_made, u - RAW + 1 + per * i)

            def load_bias(l):
                for h in range(HEADS_C):
                    for r in range(ROWS):
                        src = bass.AP(tensor=rpb.tensor,
                                      offset=((l * HEADS_C + h) * RPB_H + 7 - r) * RPB_W + 15 - (GRID_W - 1),
                                      ap=[[1, GRID_W], [RPB_W, ROWS], [1, GRID_W]])
                        q0 = GRID_W * (r % 2)
                        sp.dma_start(bias[q0:q0 + GRID_W, 2 * h + r // 2, :].rearrange("p (r c) -> p r c", r=ROWS),
                                     src).then_inc(bias_in, 16)

            def tile_units(src3, u, i, j, q):
                un = u + 4 * j + q
                slot_free(un, i, 8)
                sp.dma_start(w_raw[:, un % RAW, :].rearrange("p (k n) -> p k n", k=4),
                             src3[:, 4 * q:4 * q + 4, bass.ds((2 * i + j) * P, P)]).then_inc(raw_in[un % RAW], 16)

            def tiles(w2, col, width, u):
                src3 = w2[:, col:col + width].rearrange("(k p) n -> p k n", p=P)
                with sp.Fori(0, width // (2 * P)) as i:
                    for j in range(2):
                        for q in range(4):
                            tile_units(src3, u, i, j, q)

            def rows(w2, col, u, n=KT, k0=0):
                for k in range(k0, n):
                    slot_free(u + k)
                    sp.dma_start(w_raw[:, (u + k) % RAW, :], w2[k * P:(k + 1) * P, col:col + 512])\
                        .then_inc(raw_in[(u + k) % RAW], 16)

            def ada_row(g, n):
                h, k = n // KT, n % KT
                sp.dma_start(w_raw[:, n % RAW, :], w_ada[0, k * P:(k + 1) * P, bass.ds(D * h + 512 * g, 512)])\
                    .then_inc(raw_in[n % RAW], 16)

            for n in range(RAW):
                ada_row(0, n)
            load_bias(0)
            for n in range(RAW, 2 * KT):
                slot_free(n)
                ada_row(0, n)
            with sp.Fori(1, GROUPS) as g:
                for n in range(2 * KT):
                    sp.wait_ge(lo_made, 2 * KT * g + n - RAW + 1)
                    ada_row(g, n)

            for l in range(DEPTH):
                w2 = w_in[l]
                nq = query_tiles(l) * P
                u = PLAN["v_c", l]["unit"]
                if l == 0:
                    for j in range(4):
                        sp.wait_ge(free[j], KT // 4)
                    for g in range(4):
                        rows(w2, COL["v_c"], u, 4 * g + 4, 4 * g)
                        sp.dma_start(x_scratch[:, 4 * g:4 * g + 4, :], z[:, 4 * g:4 * g + 4, :]).then_inc(x_kept, 16)
                else:
                    rows(w2, COL["v_c"], u, KT, AHEAD)
                    load_bias(l)
                for n in ("k_c", "g_c") if l == 0 else ("q_c", "k_c", "g_c"):
                    tiles(w2, COL[n], 512, PLAN[n, l]["unit"])
                u = PLAN["v_a", l]["unit"]
                rows(w2, COL["v_a"], u, 8)
                j = PLAN["v_a", l]["att"]
                sp.wait_ge(av_done, j)
                sp.dma_start(bs_row[:, :, :], b_s[l:l + 1].broadcast_to([P, HEADS_A, P])).then_inc(gate_in, 16)
                sp.dma_start(sgu_row[:, :], sgu_g[l:l + 1, :].broadcast_to([P, W_A])).then_inc(gate_in, 16)
                sp.dma_start(ws_in[:, :, :], w_s[l].rearrange("g p q -> p g q")).then_inc(gate_in, 16)
                rows(w2, COL["v_a"], u, KT, 8)
                for n in ("u", "g_a", "cq", "ckv"):
                    tiles(w2, COL[n], 512, PLAN[n, l]["unit"])
                u = PLAN["kr", l]["unit"]
                src3 = w2[:, COL["kr"]:COL["kr"] + ROPE].rearrange("(k p) n -> p k n", p=P)
                for q in range(4):
                    slot_free(u + q)
                    dst = w_raw[:, (u + q) % RAW, :].rearrange("p (k n) -> p k n", k=4)
                    sp.dma_start(dst[:, :, 0:ROPE], src3[:, 4 * q:4 * q + 4, :]).then_inc(raw_in[(u + q) % RAW], 16)
                tiles(w2, COL["g_b"], W_B, PLAN["g_b", l]["unit"])

                u = PLAN["v_b", l]["unit"]
                for half in range(2):
                    src = w_ukv[l].rearrange("k (h n) -> k h n", h=HEADS_B)[:, 4 * half:4 * half + 4, NOPE:]
                    for k in range(KL):
                        un = u + 4 * half + k
                        slot_free(un)
                        sp.dma_start(w_raw[:, un % RAW, :].rearrange("p (h n) -> p h n", h=4),
                                     src[k * P:(k + 1) * P]).then_inc(raw_in[un % RAW], 16)
                u = PLAN["q_r", l]["unit"]
                uq3 = w_uq[l].rearrange("(k p) (h n) -> p k h n", p=P, h=HEADS_B)
                for pair in range(4):
                    slot_free(u + pair)
                    dst = w_raw[:, (u + pair) % RAW, :].rearrange("p (k n) -> p k n", k=4)
                    for half in range(2):
                        sp.dma_start(dst[:, :, half * ROPE:(half + 1) * ROPE], uq3[:, :, 2 * pair + half, NOPE:])\
                            .then_inc(raw_in[(u + pair) % RAW], 16)
                ukv3 = w_ukv[l].rearrange("(k p) (h n) -> p k h n", p=P, h=HEADS_B)
                u = PLAN["heads", l]["unit"]
                for h in range(HEADS_B):
                    for m, src in enumerate((uq3[:, :, h, 0:NOPE], ukv3[:, :, h, 0:NOPE])):
                        un = u + 2 * h + m
                        slot_free(un)
                        sp.dma_start(w_raw[:, un % RAW, :].rearrange("p (k n) -> p k n", k=4), src)\
                            .then_inc(raw_in[un % RAW], 16)

                p = PLAN["out", l]
                u = p["unit"]
                src3 = w_out[l].rearrange("(k p) n -> p k n", p=P)
                for n, (j, q) in enumerate(OUT_FIRST):
                    k = OUT_TILES[4 * q]
                    slot_free(u + n)
                    sp.dma_start(w_raw[:, (u + n) % RAW, :].rearrange("p (k n) -> p k n", k=4),
                                 src3[:, k:k + 4, j * P:(j + 1) * P]).then_inc(raw_in[(u + n) % RAW], 16)
                sp.wait_ge(x_kept, 16 * (4 + KT * l))
                sp.wait_ge(av_done, p["att"])
                for j in range(2):
                    sp.dma_start(x_res[:, j, 0:nq], x_scratch[:, j, 0:nq]).then_inc(x_back[j], 16)
                with sp.Fori(1, KT // 2) as i:
                    for j in range(2):
                        for q in range(4):
                            un = u + 4 * j + q
                            sp.wait_ge(lo_made, un - RAW + 1 + 8 * i)
                            sp.dma_start(w_raw[:, un % RAW, :].rearrange("p (k n) -> p k n", k=4),
                                         src3[:, OUT_TILES[4 * q]:OUT_TILES[4 * q] + 4, bass.ds((2 * i + j) * P, P)])\
                                .then_inc(raw_in[un % RAW], 16)
                        sp.wait_ge(free[j], p[j] + i)
                        if l == 0:
                            sp.dma_start(x_scratch[:, bass.ds(2 * i + j - 2, 1), :], z[:, bass.ds(2 * i + j - 2, 1), :])\
                                .then_inc(x_kept, 16)
                        sp.dma_start(x_res[:, j, 0:nq], x_scratch[:, bass.ds(2 * i + j, 1), 0:nq]).then_inc(x_back[j], 16)
                if l == 0:
                    rows(w_in[1], COL["v_c"], PLAN["v_c", 1]["unit"], AHEAD)
                    for j in range(2):
                        sp.wait_ge(free[j], p[j] + 8)
                        sp.dma_start(x_scratch[:, KT - 2 + j, :], z[:, KT - 2 + j, :]).then_inc(x_kept, 16)
            for g in range(4):
                tt, c0 = g // 2, (g % 2) * 1024
                for n in (2 * g, 2 * g + 1):
                    b = FINAL_BANKS[n]
                    sp.wait_ge(free[b], PLAN["end", 0][b] + FINAL_BANKS[:n + 1].count(b))
                sp.dma_start(out[0, tt * P:(tt + 1) * P, c0:c0 + 1024], y[:, tt, c0:c0 + 1024]).then_inc(out_stored, 16)
            sp.wait_ge(out_stored, 64)

        @block.gpsimd
        def _(pool):
            pool.memset(ones[:, :], 1.0).then_inc(pool_set, 1)
            pool.memset(c_st[:, :, :].bitcast(F32), 0.0).then_inc(pool_set, 1)
            keep = cst[:, C_KEEP:C_KEEP + GRID_W].unsqueeze(1).broadcast_to([P, 32, GRID_W])
            mask = cst[:, C_MASK:C_MASK + GRID_W].unsqueeze(1).broadcast_to([P, 32, GRID_W])

            def mask_bias(l):
                v = bias[:, :, :].rearrange("p a (r c) -> p (a r) c", c=GRID_W)
                pool.wait_ge(bias_in, 16 * ROWS * HEADS_C * (l + 1))
                pool.tensor_tensor(v, v, keep, ALU.mult).then_inc(bias_ready, 1)
                pool.wait_ge(bias_ready, 2 * l + 1)
                pool.tensor_tensor(v, v, mask, ALU.add).then_inc(bias_ready, 1)

            def q_row(k, c):
                pool.dma_start(ada_w[:, c, :], w_in[0, bass.ds(k * P, P), COL["q_c"]:COL["q_c"] + 512])\
                    .then_inc(ada_in[c], 16)

            for c in range(4):
                q_row(c, c)
            pool.wait_ge(const_in, 16)
            mask_bias(0)

            pool.wait_ge(free[7], 1)
            def normed(i, c):
                pool.wait_ge(free[c], i + 1)
                pool.tensor_tensor(xn[:, c:c + 1, :], z[:, bass.ds(4 * i + c, 1), :], prob[:, 0:1, :], ALU.mult)\
                    .then_inc(xn_ready, 1)

            for c in range(4):
                normed(0, c)
            def q_lo(i, c):
                pool.wait_ge(q_hi_made, 4 * i + c + 1)
                pool.tensor_tensor(q_wlo[:, c % 2, :], ada_w[:, c, :], q_whi[:, c % 2, :].bitcast(F32), ALU.subtract)\
                    .then_inc(q_lo_made, 1)

            with pool.Fori(0, KT // 4 - 1) as i:
                for c in range(4):
                    q_lo(i, c)
                    pool.wait_ge(q_lo_made, 4 * i + c + 1)
                    q_row(4 * i + 4 + c, c)
                    pool.wait_ge(op_ready, 4 * i + c + 3)
                    normed(i + 1, c)
            for c in range(4):
                q_lo(KT // 4 - 1, c)
            pool.wait_ge(q_lo_made, KT)

            def ada_rows(l, first, count, col):
                vectors, n0 = ada_vectors(first), ada_steps(first)

                def load(b, k):
                    pool.dma_start(ada_w[:, k % ADA_SLOTS, :],
                                   w_ada[l, k * P:(k + 1) * P, bass.ds(col + 512 * b, 512)])\
                        .then_inc(ada_in[k % ADA_SLOTS], 16)

                for k in range(KT):
                    if k >= ADA_SLOTS or first:
                        before = n0 + vectors * (k + 1 - ADA_SLOTS + 1)
                        if k < ADA_SLOTS:
                            before = n0 - ada_vectors(first - 1) * (ADA_SLOTS - 1 - k)
                        pool.wait_ge(ada_step, before)
                    load(0, k)
                with pool.Fori(1, count) as b:
                    n = n0 + vectors * (KT + 1) * b
                    for k in range(KT):
                        used = vectors * (k + 2 - ADA_SLOTS) if k >= ADA_SLOTS else -vectors * (ADA_SLOTS - 1 - k)
                        pool.wait_ge(ada_step, n + used)
                        load(b, k)

            def clear_kr(l):
                pool.wait_ge(av_done, PLAN["v_a", l]["att"])
                pool.memset(kr_ab[ROPE:P, 0:2, :].bitcast(F32), 0.0).then_inc(pool_set, 1)
                pool.memset(kr_ab[0:ROPE, 2:4, :].bitcast(F32), 0.0).then_inc(pool_set, 1)

            ada_rows(0, 0, 4, 2 * D)
            clear_kr(0)
            ada_rows(1, 4, 8, 0)
            mask_bias(1)
            ada_rows(1, 12, 4, 2 * D)
            clear_kr(1)

        @block.scalar
        def _(act):
            hi_n, t_n, sq_n, a_n = [0], [0], [0], [0]

            def prep(u, i=0, per=0):
                act.wait_ge(raw_in[u % RAW], 16 * (u // RAW + 1) + raw_extra(u) + 16 * (per // RAW) * i)
                if u >= RING or per:
                    act.wait_ge(unit_done, u - RING + 1 + per * i)
                dst, src = w_hi[:, u % RING, :], w_raw[:, u % RAW, :]
                if per == 0 and u in KR_UNITS:
                    dst, src = twice(dst, src)
                act.activation(dst, src, ACT.Copy).then_inc(hi_made, 1)

            def prep_ahead(u, i=0, per=0):
                if u + AHEAD < UNITS:
                    prep(u + AHEAD, i, per)

            def hi(dst, src, scale=1.0):
                hi_n[0] += 1
                act.activation(dst, src, ACT.Copy, scale=scale).then_inc(op_hi, 1)

            def tiles(name, l, evac, count=4, start=0):
                p = PLAN[name, l]
                u = p["unit"]

                def turn(i, u, per):
                    for s in range(8):
                        if s == 4:
                            evac(i, 0)
                        prep_ahead(u + s, i, per)
                    evac(i, 1)

                n = count // 2 - (name == "ckv")
                with act.Fori(start, n) as i:
                    turn(i, u, 8)
                if n < count // 2:
                    turn(n, u + 8 * n, 0)

            def tile_full(p, i, j):
                act.wait_ge(unit_done, p["unit"] + 4 * (j + 1) + 8 * i)

            act.wait_ge(free[4], 1)
            act.activation(c_silu[:, :], cols[:, Q_C:Q_C + 32], ACT.Silu).then_inc(act_step, 1)
            act.wait_ge(act_step, 1)
            act.wait_ge(pool_set, 2)
            for v in range(2):
                hi(c_st[:, :, 2 * v], c_silu[:, v * KT:(v + 1) * KT])

            for c in range(2):
                act.wait_ge(x_landed[c], 16)
                if c:
                    act.wait_ge(sq_ready, c)
                act.activation(junk[:, :], x_in[:, c, :], ACT.Square, accum_out=small[:, 50 + c:51 + c])\
                    .then_inc(sq_ready, 1)
            for u in range(AHEAD):
                prep(u)

            def rows_copy(g, h, u, i, per):
                act.wait_ge(unit_done, u + 16 * h + per * i)
                if per or 2 * g + h > 1:
                    act.wait_ge(rows_turned, 2 * g + h - 1)
                bank = 4 if h else 6
                act.activation(tmp[0:4, 3, :], ps[0:4, bank, :], ACT.Copy).then_inc(free[bank], 1)

            def chunk(g, c):
                k = 4 * g - 4 + c
                if c == 0:
                    act.wait_ge(group_ready, g)
                act.wait_ge(xn_ready, k + 1)
                for v in range(2):
                    ins = act.activation(h_hi[:, bass.ds(k, 1), v * SEQ:(v + 1) * SEQ], xn[:, c:c + 1, v * SEQ:(v + 1) * SEQ],
                                         ACT.Identity, bias=mods[:, v, bass.ds(k, 1)], scale=a_col[:, v, bass.ds(k, 1)])
                ins.then_inc(op_hi, 1)
                act.wait_ge(ada_in[c], 16 * g)
                if not isinstance(g, int) or k >= 2:
                    act.wait_ge(q_done, k - 1)
                act.activation(q_whi[:, c % 2, :], ada_w[:, c, :], ACT.Copy).then_inc(q_hi_made, 1)

            def group(g, u, i=0, per=0):
                first = isinstance(g, int) and g == 0
                for n in range(2 * KT):
                    h, s = n // KT, n % KT
                    prep(u + n + AHEAD, i, per)
                    if s == 0 and not (first and h == 0):
                        rows_copy(g, h, u, i, per)
                    if first and n < KT:
                        t = n
                        act.wait_ge(x_turned, t + 1)
                        act.activation(z[:, t, :], ps[:, t % 4, :], ACT.Copy).then_inc(free[t % 4], 1)
                    if not first and n in CHUNK_AT:
                        chunk(g, CHUNK_AT.index(n))

            group(0, 0)
            group(1, 2 * KT)
            with act.Fori(2, GROUPS) as g:
                group(g, 4 * KT, g - 2, 2 * KT)
            rows_copy(GROUPS, 0, 2 * KT * GROUPS, 0, 0)
            for c in range(4):
                chunk(GROUPS, c)
            hi_n[0] += KT
            sq_n[0] = 2
            t_n[0] = KT
            act.wait_ge(q_done, KT)
            for j in range(4):
                hi(qc_hi[:, j, :], ps[:, j, :], C_SCALE)

            def softmax_exp(j, keys):
                for qt in range(2):
                    n = 2 * j + qt
                    act.wait_ge(nmax_ready, n + 1)
                    if n >= 2:
                        act.wait_ge(prob_turned, n - 1)
                    act.activation(prob[:, qt, 0:keys], ps[:, 4 + qt, 0:keys], ACT.Exp, bias=small[:, 40 + qt:41 + qt],
                                   accum_out=small[:, 42 + qt:43 + qt]).then_inc(exp_done, 1)

            def turned_hi(j, keys, pt):
                nk = keys // P
                if j >= 1:
                    act.wait_ge(av_done, j)
                for qt in range(2):
                    act.wait_ge(prob_turned, 2 * j + qt + 1)
                    hi(pt[:, 0:nk, qt * P:(qt + 1) * P],
                       ps[:, 6 + qt, 0:keys].rearrange("p (k q) -> p k q", k=nk))

            for l in range(DEPTH):
                nt = query_tiles(l)
                nq = nt * P
                u = PLAN["v_c", l]["unit"]
                for k in range(KT):
                    if l == 0:
                        prep_ahead(u + k)
                        continue
                    t_n[0] += 1
                    act.wait_ge(t_ready, t_n[0])
                    for v in range(2):
                        hi_n[0] += v
                        ins = act.activation(h_hi[:, k, v * SEQ:(v + 1) * SEQ], tmp[:, k % 2, v * SEQ:(v + 1) * SEQ],
                                             ACT.Identity, bias=mods[:, v, 48 * l + k:48 * l + k + 1])
                    ins.then_inc(op_hi, 1)
                    if k >= 2:
                        prep_ahead(u + k - 2)
                if l:
                    prep_ahead(u + KT - 2)
                    prep_ahead(u + KT - 1)
                act.wait_ge(unit_done, u + KT)
                for tt in range(4):
                    hi(vc_hi[:, tt, :], ps[:, V_C_BANK[l] + tt, :])

                def q_tile(i, j):
                    tile_full(PLAN["q_c", l], i, j)
                    act.activation(qc_hi[:, bass.ds(2 * i + j, 1), 0:nq], ps[:, j, 0:nq], ACT.Copy, scale=C_SCALE)\
                        .then_inc(op_hi, 1)

                def k_tile(i, j):
                    tile_full(PLAN["k_c", l], i, j)
                    act.activation(kc_hi[:, bass.ds(2 * i + j, 1), :], ps[:, j, :], ACT.Copy).then_inc(op_hi, 1)

                def gate_tile(name, first, func=ACT.Silu):
                    def evac(i, j):
                        tile_full(PLAN[name, l], i, j)
                        act.activation(z[:, bass.ds(first + 2 * i + j, 1), 0:nq], ps[:, j, 0:nq], func)\
                            .then_inc(free[j], 1)
                    return evac

                if l:
                    tiles("q_c", l, q_tile)
                    hi_n[0] += 4
                act.wait_ge(x_kept, 16 * (4 + KT * l))
                tiles("k_c", l, k_tile)
                hi_n[0] += 4
                tiles("g_c", l, gate_tile("g_c", 12))

                jobs = att_jobs(l, HEADS_C)
                j0 = PLAN["att_c", l]["att"]
                for r in range(-1, len(jobs)):
                    if r + 1 < len(jobs):
                        _, q0, k0 = jobs[r + 1]
                        softmax_exp(j0 + r + 1, TOK - k0)
                    if r >= 0:
                        turned_hi(j0 + r, TOK - jobs[r][2], ptc_hi)

                u = PLAN["v_a", l]["unit"]
                for k in range(KT):
                    prep_ahead(u + k)
                act.wait_ge(unit_done, u + KT)
                for tt in range(nt):
                    act.activation(z[:, VA + tt, :], ps[:, tt, :], ACT.Gelu_apprx_tanh).then_inc(free[tt], 1)
                tiles("u", l, gate_tile("u", UG, ACT.Gelu_apprx_tanh))
                tiles("g_a", l, gate_tile("g_a", 0))

                def raw_tile(name, first, n):
                    sq0 = sq_n[0]
                    def evac(i, j):
                        tile_full(PLAN[name, l], i, j)
                        act.wait_ge(op_ready, PLAN["cq", l]["ready"])
                        act.wait_ge(sq_sum, sq0 + j - 1 + 2 * i)
                        act.activation(tmp[:, j, 0:n], ps[:, j, 0:n], ACT.Square).then_inc(sq_ready, 1)
                        act.activation(z[:, bass.ds(first + 2 * i + j, 1), 0:n], ps[:, j, 0:n], ACT.Copy)\
                            .then_inc(free[j], 1)
                    return evac

                tiles("cq", l, raw_tile("cq", RAWL, nq))
                sq_n[0] += 4
                tiles("ckv", l, raw_tile("ckv", RAWL + KL, TOK))
                sq_n[0] += 4

                p = PLAN["kr", l]
                for q in range(4):
                    prep_ahead(p["unit"] + q)
                act.wait_ge(unit_done, p["unit"] + 4)
                act.activation(prob[:, 0, :], ps[:, 2, :], ACT.Copy).then_inc(free[2], 1)

                u = PLAN["g_b", l]["unit"]
                g_b = gate_tile("g_b", 4)
                for m in range(16):
                    if m % 4 == 0 and m:
                        g_b(m // 4 // 3, (m // 4 - 1) % 2)
                    if m % 2 == 0:
                        s = m // 2
                        t_n[0] += 1
                        act.wait_ge(t_ready, t_n[0])
                        n = nq if s < KL else TOK
                        hi((cq_hi if s < KL else cv_hi)[:, s % KL, 0:n], tmp[:, 2 + s % 2, 0:n])
                    prep_ahead(u + m)
                t_n[0] += 1
                act.wait_ge(t_ready, t_n[0])
                hi(kr_ab[0:ROPE, 0, :], prob[0:ROPE, 0, :])
                hi(kr_ab[ROPE:P, 2, :], prob[ROPE:P, 0, :])
                g_b(1, 1)
                tiles("g_b", l, g_b, 8, 2)

                u = PLAN["v_b", l]["unit"]
                for half in range(2):
                    for k in range(KL):
                        prep_ahead(u + 4 * half + k)
                    act.wait_ge(unit_done, u + 4 * half + 4)
                    for tt in range(4):
                        hi(v_hi[:, tt, half * 512:half * 512 + 512], ps[:, 4 * half + tt, :])

                u = PLAN["q_r", l]["unit"]
                t0 = t_n[0]
                for pair in range(5):
                    if pair < 4:
                        prep_ahead(u + pair)
                        act.wait_ge(unit_done, u + pair + 1)
                        if pair >= 2:
                            act.wait_ge(t_ready, t0 + pair - 1)
                        act.activation(prob[:, pair % 2, 0:nq], ps[:, pair % 2, 0:nq], ACT.Copy)\
                            .then_inc(free[pair % 2], 1)
                    if pair >= 1:
                        t_n[0] += 1
                        act.wait_ge(t_ready, t_n[0])
                        hi(qr_hi[:, pair - 1, 0:nq], tmp[:, 2 + (pair - 1) % 2, 0:nq])

                u = PLAN["heads", l]["unit"]

                def head_operands(h):
                    prep_ahead(u + 2 * h)
                    act.wait_ge(unit_done, u + 2 * h + 1)
                    hi(qk_hi[:, h % 2, 0:nq], ps[:, 0, 0:nq], MLA_SCALE)
                    prep_ahead(u + 2 * h + 1)
                    act.wait_ge(unit_done, u + 2 * h + 2)
                    hi(qk_hi[:, 2 + h % 2, :], ps[:, 1, :])

                jobs = att_jobs(l, HEADS_B)
                j0 = PLAN["heads", l]["att"]
                p = PLAN["out", l]
                for b in (2, 3):
                    act.wait_ge(free[b], PLAN["heads", l][b])
                head_operands(0)
                for r in range(-1, len(jobs)):
                    if r + 1 < len(jobs):
                        h, q0, k0 = jobs[r + 1]
                        if q0 == 0 and h + 1 < HEADS_B:
                            head_operands(h + 1)
                        softmax_exp(j0 + r + 1, TOK - k0)
                    if r >= 0:
                        turned_hi(j0 + r, TOK - jobs[r][2], ptb_hi)
                        for m in early_tiles(l, r):
                            if m == 0:
                                act.wait_ge(unit_done, p["unit"])
                            hi(oa_hi[:, m, 0:nq], z[:, OUT_TILES[m], 0:nq])

                u = p["unit"]
                for n in range(2):
                    prep_ahead(u + n)
                for m in range(8):
                    if m in (0, 7):
                        for b in (2, 3):
                            act.wait_ge(free[b], p[b] - (m == 0 and b == 2 + (len(jobs) - 1) % 2))
                    hi(ob_hi[:, m, 0:nq], z[:, OUT_TILES[8 + m], 0:nq])
                    if m % 4 == 3:
                        prep_ahead(u + 2 + m // 4)
                sq0 = sq_n[0]

                def new_x(i, j):
                    act.wait_ge(free[j], p[j] + 1 + i)
                    act.wait_ge(sq_sum, sq0 + j - 1 + 2 * i)
                    t = bass.ds(2 * i + j, 1)
                    act.activation(tmp[:, j, 0:nq], z[:, t, 0:nq], ACT.Square).then_inc(sq_ready, 1)
                    if l == DEPTH - 1:
                        act.activation(xg[:, t, :], z[:, t, 0:SEQ], ACT.Copy,
                                       scale=cols[:, bass.ds(Q_FG + 2 * i + j, 1)]).then_inc(xg_ready, 1)

                for s in range(4, 8):
                    prep_ahead(u + s)
                new_x(0, 0)
                if l == 0:
                    with act.Fori(1, KT // 2) as i:
                        for s in range(8):
                            if s == 1:
                                new_x(i - 1, 1)
                            if s == 5:
                                new_x(i, 0)
                            prep_ahead(u + s, i, 8)
                else:
                    with act.Fori(1, KT // 2 - 1) as i:
                        for s in range(8):
                            if s == 1:
                                new_x(i - 1, 1)
                            if s == 5:
                                new_x(i, 0)
                            prep_ahead(u + s, i, 8)
                    i = KT // 2 - 1
                    for s in range(8):
                        if s == 1:
                            new_x(i - 1, 1)
                        if s == 5:
                            new_x(i, 0)
                        prep_ahead(u + 8 * i + s)
                new_x(KT // 2 - 1, 1)
                sq_n[0] += KT

            p = PLAN["end", 0]
            act.wait_ge(final_rms, 1)
            for n in range(1, 8, 2):
                tt, g, b = n // 4, n % 4, FINAL_BANKS[n]
                act.wait_ge(job_done, p["job"] + (n + 1 if n < 4 else n + 2))
                act.activation(y[:, tt, g * 512:(g + 1) * 512], ps[:, b, :], ACT.Copy, scale=small[:, 10 + tt:11 + tt])\
                    .then_inc(free[b], 1)

        @block.tensor
        def _(pe):
            def wait_unit(u, i=0, per=0):
                pe.wait_ge(lo_made, u + 1 + per * i)

            def split_mm(dst, a_hi, a_lo, b_hi, b_lo, first, last):
                pe.matmul(dst, a_lo, b_hi, start=first, stop=False)
                pe.matmul(dst, a_hi, b_lo, start=False, stop=False)
                return pe.matmul(dst, a_hi, b_hi, start=False, stop=last)

            def turn(dst, src, n=P):
                return pe.transpose(dst, src, ident[0:n, 0:n])

            def stationary_unit(dst, u, b_hi, b_lo, k0, cols_n, first, last):
                s = u % RING
                for kk in range(4):
                    w = slice(kk * P, (kk + 1) * P)
                    mm = split_mm(dst, w_hi[:, s, w], w_lo[:, s, w], b_hi[:, k0 + kk, 0:cols_n],
                                  b_lo[:, k0 + kk, 0:cols_n], first and kk == 0, last and kk == 3)
                mm.then_inc(unit_done, 1)

            def tiles(name, l, n, count=4):
                p = PLAN[name, l]
                u = p["unit"]
                with pe.Fori(0, count // 2) as i:
                    for j in range(2):
                        pe.wait_ge(free[j], p[j] + i)
                        for q in range(4):
                            wait_unit(u + 4 * j + q, i, 8)
                            stationary_unit(ps[:, j, 0:n], u + 4 * j + q, h_hi, h_lo, 4 * q, n, q == 0, q == 3)

            def moving_unit(u, a_hi, a_lo, k, nt, first, last, bank=0):
                s = u % RING
                for tt in range(nt):
                    t = slice(tt * P, (tt + 1) * P)
                    mm = split_mm(ps[:, bank + tt, :], a_hi[:, k, t], a_lo[:, k, t], w_hi[:, s, :], w_lo[:, s, :],
                                  first, last)
                mm.then_inc(unit_done, 1)

            def ada(l, after):
                if (("ada", after), l) not in PLAN.at:
                    return
                p = PLAN[("ada", after), l]
                b = ada_bank(l, after)
                pe.wait_ge(ada_step, ada_steps(p["ada"] + 1))
                for v in range(ada_vectors(p["ada"])):
                    pe.wait_ge(free[b + v], p[b + v])
                    for c in range(4):
                        mm = turn(ps[:, b + v, c * P:(c + 1) * P], ada_acc[:, v, c * P:(c + 1) * P])
                mm.then_inc(ada_taken, 1)

            pe.wait_ge(const_in, 16)
            pe.wait_ge(rows_in, 32)
            turn(ps[:, 4, 0:96], tmp[0:96, 0, 0:P], 96).then_inc(job_done, 1)
            turn(ps[:, 5, 0:96], tmp[0:96, 1, 0:P], 96).then_inc(job_done, 1)

            def turn_rows_of(g, h):
                if h:
                    pe.wait_ge(free[4], g + 2)
                else:
                    pe.wait_ge(free[6], g)
                pe.wait_ge(free[5], 2 * g + h)
                for c in range(4):
                    mm = pe.matmul(ps[:, 5, 4 * c:4 * c + 4], tmp[0:4, 3, c * P:(c + 1) * P], ident[0:4, 0:4],
                                   start=True, stop=True)
                mm.then_inc(rows_turned, 1)

            def q_unit(g, c):
                k = 4 * g - 5 + c
                c = (c - 1) % 4
                if isinstance(g, int) and k < 0:
                    return
                if isinstance(g, int) and k == 0:
                    for j in range(4):
                        pe.wait_ge(free[j], KT // 4)
                pe.wait_ge(q_lo_made, k + 1)
                pe.wait_ge(op_ready, k + 3)
                t = bass.ds(k, 1)
                for j in range(4):
                    w = slice(j * P, (j + 1) * P)
                    mm = split_mm(ps[:, j:j + 1, :], q_whi[:, c % 2, w], q_wlo[:, c % 2, w], h_hi[:, t, :], h_lo[:, t, :],
                                  isinstance(g, int) and k == 0, isinstance(g, int) and k == KT - 1)
                mm.then_inc(q_done, 1)

            def group(g, u, i=0, per=0):
                first = isinstance(g, int) and g == 0
                for n in range(2 * KT):
                    h, s = n // KT, n % KT
                    if first and n < KT:
                        t = n
                        if t == 0:
                            for tt in range(4):
                                pe.wait_ge(x_landed[tt], 16)
                        if t >= 4:
                            pe.wait_ge(free[t % 4], t // 4)
                        for tt in range(4):
                            mm = turn(ps[:, t % 4, tt * P:(tt + 1) * P], x_in[:, tt, t * P:(t + 1) * P])
                        mm.then_inc(x_turned, 1)
                    if s == 3 and not (first and h == 0):
                        turn_rows_of(g, h)
                    if first and n == 5:
                        pe.wait_ge(sq_sum, 2)
                        pe.matmul(ps[:, 7, :], ones[:, :], tmp[:, 2, :], start=True, stop=True).then_inc(job_done, 1)
                    wait_unit(u + n, i, per)
                    if s == 0 and h == 0:
                        pe.wait_ge(free[4], g + 1)
                    elif s == 0 and not first:
                        pe.wait_ge(free[6], g)
                    bank = 6 if h else 4
                    pe.matmul(ps[:, bank, :], c_st[:, s, :], w_lo[:, n % RING, :], start=s == 0, stop=False)
                    pe.matmul(ps[:, bank, :], c_st[:, s, :], w_hi[:, n % RING, :], start=False, stop=s == KT - 1)\
                        .then_inc(unit_done, 1)
                    if not first and n in CHUNK_AT:
                        q_unit(g, CHUNK_AT.index(n))

            pe.wait_ge(op_ready, 2)
            group(0, 0)
            group(1, 2 * KT)
            with pe.Fori(2, GROUPS) as g:
                group(g, 4 * KT, g - 2, 2 * KT)
            turn_rows_of(GROUPS, 0)
            for c in range(5):
                q_unit(GROUPS, c)

            for l in range(DEPTH):
                nt = query_tiles(l)
                nq = nt * P
                if l:
                    p = PLAN["head", l]
                    pe.wait_ge(sq_sum, p["sq"])
                    for c in range(4):
                        mm = pe.matmul(ps[:, 4, c:c + 1], tmp[:, 2, c * P:(c + 1) * P], ones[:, 0:1],
                                       start=True, stop=True)
                    mm.then_inc(job_done, 1)
                    pe.wait_ge(op_ready, p["ready"] + 1)
                    pe.matmul(ps[:, 5, :], ones[:, :], tmp[:, 3, :], start=True, stop=True).then_inc(job_done, 1)

                u, bank = PLAN["v_c", l]["unit"], V_C_BANK[l]
                for k in range(KT):
                    wait_unit(u + k)
                    if l:
                        pe.wait_ge(op_ready, p["ready"] + 2 + k)
                    if k == 0:
                        for b in range(bank, bank + 4):
                            pe.wait_ge(free[b], PLAN["v_c", l][b])
                    moving_unit(u + k, h_hi, h_lo, k, 4, k == 0, k == KT - 1, bank)
                ada(l, "v_c")
                for n, w in (("q_c", nq), ("k_c", TOK), ("g_c", nq))[0 if l else 1:]:
                    tiles(n, l, w)
                    if n != "g_c":
                        ada(l, n)

                def scores(j, terms, keys, bias_of=None):
                    for qt in range(2):
                        if j >= 1:
                            pe.wait_ge(exp_done, 2 * j + qt - 1)
                        for n, (qh, ql, kh, kl, q0, k0) in enumerate(terms):
                            q = slice(q0 + qt * P, q0 + (qt + 1) * P)
                            k, dst = slice(k0, k0 + keys), ps[:, 4 + qt, 0:keys]
                            pe.matmul(dst, ql[:, q], kh[:, k], start=n == 0, stop=False)
                            if bias_of is not None:
                                pe.matmul(ps[:, 4 + qt, 0:SEQ], turn_rows, bias[:, 2 * bias_of + qt, :],
                                          start=False, stop=False)
                            pe.matmul(dst, qh[:, q], kl[:, k], start=False, stop=False)
                            mm = pe.matmul(dst, qh[:, q], kh[:, k], start=False, stop=n == len(terms) - 1)
                        mm.then_inc(scores_done, 1)

                def turn_probs(p, r, keys):
                    for qt in range(2):
                        pe.wait_ge(prob_ready, 2 * (p["att"] + r) + qt + 1)
                        pe.wait_ge(free[6 + qt], p[6 + qt] + r)
                        for c in range(keys // P):
                            mm = turn(ps[:, 6 + qt, c * P:(c + 1) * P], prob[:, qt, c * P:(c + 1) * P])
                        mm.then_inc(prob_turned, 1)

                def apply_values(p, r, keys, k0, vh, vl, c0, pt_hi, pt_lo):
                    b = 2 + r % 2
                    pe.wait_ge(free[b], p[b] + r // 2)
                    for qt in range(2):
                        pe.wait_ge(free[6 + qt], p[6 + qt] + r + 1)
                    nk = keys // P
                    for c in range(nk):
                        t = k0 // P + c
                        mm = split_mm(ps[:, b, 0:256], vh[:, t, c0:c0 + P], vl[:, t, c0:c0 + P],
                                      pt_hi[:, c, :], pt_lo[:, c, :], c == 0, c == nk - 1)
                    mm.then_inc(av_done, 1)

                jobs = att_jobs(l, HEADS_C)
                p = PLAN["att_c", l]
                pe.wait_ge(bias_ready, 2 * l + 2)
                pe.wait_ge(free[4], p[4])
                pe.wait_ge(free[5], p[5])
                pe.wait_ge(free[0], p[0])
                pe.wait_ge(free[1], p[1])
                for r in range(-1, len(jobs) + 1):
                    if r + 1 < len(jobs):
                        h, q0, k0 = jobs[r + 1]
                        scores(p["att"] + r + 1, [(qc_hi[:, h], qc_lo[:, h], kc_hi[:, h], kc_lo[:, h], q0, k0)],
                               TOK - k0, h if q0 == 0 else None)
                    if 0 <= r < len(jobs):
                        turn_probs(p, r, TOK - jobs[r][2])
                    if r >= 1:
                        h, q0, k0 = jobs[r - 1]
                        apply_values(p, r - 1, TOK - k0, k0, vc_hi, vc_lo, h * P, ptc_hi, ptc_lo)

                ada(l, "g_c")
                p = PLAN["v_a", l]
                for k in range(KT):
                    wait_unit(p["unit"] + k)
                    if k == 0:
                        for tt in range(nt):
                            pe.wait_ge(free[tt], p[tt])
                    moving_unit(p["unit"] + k, h_hi, h_lo, k, nt, k == 0, k == KT - 1)
                p = PLAN["w_s", l]
                pe.wait_ge(gate_in, 48 * (l + 1))
                for g in range(4):
                    mm = turn(ps[:, 4, g * P:(g + 1) * P], ws_in[:, g, :])
                mm.then_inc(job_done, 1)
                ada(l, "v_a")
                for n in ("u", "g_a"):
                    tiles(n, l, nq)
                    ada(l, n)

                p = PLAN["mix_a", l]
                pe.wait_ge(op_ready, p["ready"])
                for g in range(4):
                    pe.wait_ge(free[2 + g], p[2 + g])
                    for tt in range(nt):
                        mm = pe.matmul(ps[:, 2 + g, tt * P:(tt + 1) * P], z[:, VA + tt, g * P:(g + 1) * P],
                                       ws_t[:, g, :], start=True, stop=True)
                    mm.then_inc(job_done, 1)

                tiles("cq", l, nq)
                ada(l, "cq")
                tiles("ckv", l, TOK)
                ada(l, "ckv")

                p = PLAN["lat", l]
                pe.wait_ge(sq_sum, p["sq"])
                for c in range(nt + 4):
                    src = tmp[:, 2, c * P:(c + 1) * P] if c < nt else tmp[:, 3, (c - nt) * P:(c - nt + 1) * P]
                    mm = pe.matmul(ps[:, 4, c:c + 1], src, ones[:, 0:1], start=True, stop=True)
                mm.then_inc(job_done, 1)
                k = PLAN["kr", l]
                pe.wait_ge(free[2], k[2])
                for q in range(4):
                    wait_unit(k["unit"] + q)
                    stationary_unit(ps[:, 2, :], k["unit"] + q, h_hi, h_lo, 4 * q, TOK, q == 0, q == 3)
                pe.wait_ge(op_ready, p["ready"] + 1)
                pe.matmul(ps[:, 5, 0:nq], ones[:, :], tmp[:, 0, 0:nq], start=True, stop=True).then_inc(job_done, 1)
                pe.wait_ge(op_ready, p["ready"] + 2)
                pe.matmul(ps[:, 4, :], ones[:, :], tmp[:, 1, :], start=True, stop=True).then_inc(job_done, 1)
                pe.wait_ge(free[2], k[2] + 1)
                pe.wait_ge(free[3], k[3])
                pe.matmul(ps[:, 3, 0:SEQ], rot, prob[:, 0, 0:SEQ], start=True, stop=True).then_inc(job_done, 1)
                tiles("g_b", l, nq, 8)

                p = PLAN["v_b", l]
                pe.wait_ge(op_ready, p["ready"])
                for half in range(2):
                    for b in range(4 * half, 4 * half + 4):
                        pe.wait_ge(free[b], (PLAN["v_b2", l] if half else p)[b])
                    for k in range(KL):
                        un = p["unit"] + 4 * half + k
                        if (half, k) == (0, 2):
                            ada(l, "g_b")
                        wait_unit(un)
                        moving_unit(un, cv_hi, cv_lo, k, 4, k == 0, k == KL - 1, 4 * half)
                p = PLAN["q_r", l]
                for pair in range(5):
                    if pair < 4:
                        wait_unit(p["unit"] + pair)
                        pe.wait_ge(free[pair % 2], p[pair % 2] + pair // 2)
                        stationary_unit(ps[:, pair % 2, 0:nq], p["unit"] + pair, cq_hi, cq_lo, 0, nq, True, True)
                    if pair >= 1:
                        m = pair - 1
                        pe.wait_ge(free[m % 2], p[m % 2] + m // 2 + 1)
                        pe.wait_ge(free[2 + m % 2], p[2 + m % 2] + m // 2)
                        pe.matmul(ps[:, 2 + m % 2, 0:SEQ], rot, prob[:, m % 2, 0:SEQ], start=True, stop=True)\
                            .then_inc(job_done, 1)

                p = PLAN["heads", l]

                def head_operands(h):
                    for m, (bh, bl, n) in enumerate(((cq_hi, cq_lo, nq), (cv_hi, cv_lo, TOK))):
                        un = p["unit"] + 2 * h + m
                        wait_unit(un)
                        pe.wait_ge(free[m], p[m] + h)
                        stationary_unit(ps[:, m, 0:n], un, bh, bl, 0, n, True, True)

                out_u, out_p = PLAN["out", l]["unit"], PLAN["out", l]

                def out_unit(n, bank, q, i=0, per=0):
                    wait_unit(n, i, per)
                    bh, bl = (oa_hi, oa_lo) if q < 2 else (ob_hi, ob_lo)
                    stationary_unit(ps[:, bank, 0:nq], n, bh, bl, 4 * (q % 2), nq, q == 0, q == 3)

                def out_first(n):
                    j, q = OUT_FIRST[n]
                    if q == 0:
                        pe.wait_ge(free[j], out_p[j])
                    pe.wait_ge(op_ready, out_p["ready"] + 4 * q + 4)
                    out_unit(out_u + n, j, q)

                jobs = att_jobs(l, HEADS_B)
                head_operands(0)
                pe.wait_ge(op_ready, p["ready"])
                pe.wait_ge(pool_set, 2 * l + 4)
                pe.wait_ge(free[4], p[4])
                pe.wait_ge(free[5], p[5])
                for r in range(-1, len(jobs) + 1):
                    if r + 1 < len(jobs):
                        h, q0, k0 = jobs[r + 1]
                        if q0 == 0 and h + 1 < HEADS_B:
                            head_operands(h + 1)
                        if q0 == 0:
                            pe.wait_ge(free[0], p[0] + h + 1)
                            pe.wait_ge(free[1], p[1] + h + 1)
                        e = 2 * (h % 2)
                        scores(p["att"] + r + 1, [
                            (qk_hi[:, h % 2], qk_lo[:, h % 2], qk_hi[:, 2 + h % 2], qk_lo[:, 2 + h % 2], q0, k0),
                            (qr_hi[:, h // 2], qr_lo[:, h // 2], kr_ab[:, e], kr_ab[:, e + 1], q0, k0)], TOK - k0)
                    if r == len(jobs) - 1:
                        out_first(0)
                    if 0 <= r < len(jobs):
                        turn_probs(p, r, TOK - jobs[r][2])
                    if r == len(jobs):
                        out_first(1)
                    if r >= 1:
                        h, q0, k0 = jobs[r - 1]
                        apply_values(p, r - 1, TOK - k0, k0, v_hi, v_lo, h * P, ptb_hi, ptb_lo)

                p = PLAN["out", l]
                u = p["unit"]
                for n in range(2, 8):
                    out_first(n)
                for first, end in ((1, 3), (3, 5), (5, 7), (7, 8)) if l == 0 else ((1, 8),):
                    with pe.Fori(first, end) as i:
                        for j in range(2):
                            pe.wait_ge(free[j], p[j] + i)
                            for q in range(4):
                                out_unit(u + 4 * j + q, j, q, i, 8)
                    if end < 8:
                        ada(l, f"out{first}")

            p = PLAN["end", 0]
            for n in range(8):
                tt, g = n // 4, n % 4
                b = FINAL_BANKS[n]
                pe.wait_ge(xg_ready, 4 * g + 4 if tt == 0 else KT)
                pe.wait_ge(free[b], p[b] + (1 if n >= 6 else 0))
                for c in range(4):
                    mm = turn(ps[:, b, c * P:(c + 1) * P], xg[:, 4 * g + c, tt * P:(tt + 1) * P])
                mm.then_inc(job_done, 1)
                if n == 3:
                    pe.wait_ge(sq_sum, p["sq"])
                    for c in range(2):
                        mm = pe.matmul(ps[:, 4, c:c + 1], tmp[:, 2, c * P:(c + 1) * P], ones[:, 0:1],
                                       start=True, stop=True)
                    mm.then_inc(job_done, 1)

        @block.vector
        def _(dve):
            step, hi_n, t_n, sq_n = [0], [0], [0], [0]

            def link(ins):
                step[0] += 1
                ins.then_inc(dve_step, 1)
                dve.wait_ge(dve_step, step[0])

            def prep(u, i=0, per=0):
                dve.wait_ge(hi_made, u + 1 + per * i)
                dst, src, top = w_lo[:, u % RING, :], w_raw[:, u % RAW, :], w_hi[:, u % RING, :]
                if per == 0 and u in KR_UNITS:
                    (dst, src), (top, _) = twice(dst, src), twice(top, src)
                dve.tensor_tensor(dst, src, top.bitcast(F32), ALU.subtract).then_inc(lo_made, 1)

            def prep_ahead(u, i=0, per=0):
                if u + AHEAD < UNITS:
                    prep(u + AHEAD, i, per)

            def next_hi():
                hi_n[0] += 1
                dve.wait_ge(op_hi, hi_n[0])

            def lo(dst, src, hi, scale=None):
                next_hi()
                if scale is None:
                    return dve.tensor_tensor(dst, src, hi.bitcast(F32), ALU.subtract)
                return dve.scalar_tensor_tensor(out=dst, in0=src, scalar=scale, in1=hi.bitcast(F32),
                                                op0=ALU.mult, op1=ALU.subtract)

            def rsqrt(n, told=None):
                v, r, t = small[:, 0:n], small[:, 10:10 + n], small[:, 20:20 + n]
                link(dve.tensor_single_scalar(t.bitcast(I32), v.bitcast(I32), 1, ALU.logical_shift_right))
                link(dve.tensor_scalar(r.bitcast(I32), t.bitcast(I32), -1.0, float(0x5F3759DF), ALU.mult, ALU.add))
                for newton in range(3):
                    link(dve.tensor_tensor(t, r, r, ALU.mult))
                    link(dve.scalar_tensor_tensor(out=t, in0=t, scalar=-0.5, in1=v, op0=ALU.mult, op1=ALU.mult))
                    ins = dve.scalar_tensor_tensor(out=r, in0=t, scalar=1.5, in1=r, op0=ALU.add, op1=ALU.mult)
                    if told is None or newton < 2:
                        link(ins)
                if told is not None:
                    ins.then_inc(told, 1)
                    dve.wait_ge(told, 1)

            def mean_square(n, width, bank):
                link(dve.tensor_scalar(small[:, 0:n], ps[:, bank, 0:n], 1.0 / width, EPS, ALU.mult, ALU.add))

            def ada_block(l, name):
                if (("ada", name), l) not in PLAN.at:
                    return None
                block = PLAN[("ada", name), l]["ada"]
                if block:
                    dve.wait_ge(ada_taken, block)
                for v in range(ada_vectors(block)):
                    dve.memset(ada_acc[:, v, :], 0.0).then_inc(ada_step, 1)
                return block

            def ada_add(block, s, i=0):
                if block is None:
                    return
                nv = ada_vectors(block)
                dve.wait_ge(ada_in[s % ADA_SLOTS], 16 * (4 + 4 * block + s // ADA_SLOTS + 1) + 32 * i)
                for v in range(nv):
                    dve.wait_ge(ada_step, ada_steps(block) + nv * s + v + 1 + 8 * nv * i)
                    dve.scalar_tensor_tensor(out=ada_acc[:, v, :], in0=ada_w[:, s % ADA_SLOTS, :],
                                             scalar=c_silu[:, bass.ds(v * KT + s + 8 * i, 1)],
                                             in1=ada_acc[:, v, :], op0=ALU.mult, op1=ALU.add).then_inc(ada_step, 1)

            def tiles(name, l, evac, count=4, start=0, between=None):
                u = PLAN[name, l]["unit"]
                block = ada_block(l, name)

                def turn(i, u, per, block=None):
                    for s in range(8):
                        if s == 4 and evac:
                            evac(i, 0)
                        prep_ahead(u + s, i, per)
                        ada_add(block, s, i - start)
                        if between:
                            between(8 * i + s)
                    if evac:
                        evac(i, 1)

                if name == "ckv" or between:
                    turn(0, u, 0, block)
                    turn(1, u + 8, 0, block)
                    return
                with dve.Fori(start, start + 2) as i:
                    turn(i, u, 8, block)
                if start + 2 < count // 2:
                    with dve.Fori(start + 2, count // 2) as i:
                        turn(i, u, 8)

            def ada(l, after):
                if (("ada", after), l) not in PLAN.at:
                    return
                p = PLAN[("ada", after), l]
                c = 2 * KT + 4 * p["ada"]
                dve.wait_ge(ada_taken, p["ada"] + 1)
                b = ada_bank(l, after)
                nv = ada_vectors(p["ada"])
                for v in range(nv):
                    dve.tensor_reduce(mods[:, v, c:c + 4], ps[:, b + v, :].rearrange("p (c k) -> p c k", c=4),
                                      AX.X, ALU.add).then_inc(free[b + v], 1)
                for v in range(nv):
                    dve.wait_ge(free[b + v], p[b + v] + 1)
                link(dve.tensor_tensor(mods[:, 0:nv, c:c + 4], mods[:, 0:nv, c:c + 4],
                                       cols[:, Q_BADA + c:Q_BADA + c + 4].unsqueeze(1).broadcast_to([P, nv, 4]), ALU.add))

            dve.wait_ge(job_done, 1)
            dve.tensor_copy(cols[:, 0:Q_BADA], ps[:, 4, 0:96]).then_inc(free[4], 1)
            dve.wait_ge(job_done, 2)
            dve.tensor_copy(cols[:, Q_BADA:Q_N], ps[:, 5, 0:96]).then_inc(free[5], 1)
            dve.wait_ge(op_hi, 2)
            for v in range(2):
                dve.tensor_tensor(c_st[:, :, 2 * v + 1], c_silu[:, v * KT:(v + 1) * KT],
                                  c_st[:, :, 2 * v].bitcast(F32), ALU.subtract).then_inc(op_ready, 1)
            hi_n[0] = 2
            for c in (2, 3):
                dve.wait_ge(x_landed[c], 16)
                link(dve.tensor_tensor_reduce(tmp[:, :, :].rearrange("p a n -> p (a n)"), x_in[:, c, :], x_in[:, c, :],
                                              1.0, 0.0, ALU.mult, ALU.add, small[:, 50 + c:51 + c]))
            for u in range(AHEAD):
                prep(u)

            def columns_of(g, h):
                dve.wait_ge(rows_turned, 2 * g + h)
                c = 4 * g if h else 4 * g - 4
                m = mods[:, :, bass.ds(c if h else KT + c, 4)]
                dve.tensor_reduce(m.rearrange("p v c -> p c v"),
                                  ps[:, 5, 0:16].rearrange("p (c v k) -> p c v k", c=4, v=2), AX.X, ALU.add)\
                    .then_inc(free[5], 1)
                dve.wait_ge(free[5], 2 * g + h + 1)
                dve.tensor_tensor(m, m, cols[:, bass.ds(Q_BADA + (0 if h else KT) + c, 4)].unsqueeze(1)
                                  .broadcast_to([P, 2, 4]), ALU.add).then_inc(mod_step, 1)
                if not h:
                    dve.wait_ge(mod_step, 2 * g)
                    dve.scalar_tensor_tensor(out=a_col[:, :, bass.ds(c, 4)], in0=m, scalar=1.0,
                                             in1=cols[:, bass.ds(Q_NG + c, 4)].unsqueeze(1).broadcast_to([P, 2, 4]),
                                             op0=ALU.add, op1=ALU.mult).then_inc(group_ready, 1)

            def chunk(g, c):
                k = 4 * g - 4 + c
                if c == 0:
                    dve.wait_ge(group_ready, g)
                dve.wait_ge(xn_ready, k + 1)
                if not isinstance(g, int) or k >= 2:
                    dve.wait_ge(op_ready, k + 1)
                for v in range(2):
                    ins = dve.tensor_scalar(tmp[:, c % 2, v * SEQ:(v + 1) * SEQ], xn[:, c, v * SEQ:(v + 1) * SEQ],
                                            a_col[:, v, bass.ds(k, 1)], mods[:, v, bass.ds(k, 1)], ALU.mult, ALU.add)
                ins.then_inc(t_ready, 1)
                dve.wait_ge(t_ready, k + 1)
                dve.wait_ge(op_hi, k + 3)
                dve.tensor_tensor(h_lo[:, bass.ds(k, 1), :], tmp[:, c % 2:c % 2 + 1, :],
                                  h_hi[:, bass.ds(k, 1), :].bitcast(F32), ALU.subtract).then_inc(op_ready, 1)

            def group(g, u, i=0, per=0):
                first = isinstance(g, int) and g == 0
                for n in range(2 * KT):
                    h, s = n // KT, n % KT
                    prep(u + n + AHEAD, i, per)
                    if s == 3 and not (first and h == 0):
                        columns_of(g, h)
                    if first and n == 1:
                        dve.wait_ge(sq_ready, 2)
                        link(dve.tensor_scalar(small[:, 0:4], small[:, 50:54], 1.0 / D, EPS, ALU.mult, ALU.add))
                        rsqrt(4)
                        for c in range(4):
                            ins = dve.tensor_scalar(tmp[:, 2, c * P:(c + 1) * P], ident, small[:, 10 + c:11 + c], None, ALU.mult)
                            if c % 2:
                                ins.then_inc(sq_sum, 1)
                    if first and n == 7:
                        dve.wait_ge(job_done, 3)
                        dve.tensor_copy(prob[:, 0, :], ps[:, 7, :]).then_inc(free[7], 1)
                    if not first and n in CHUNK_AT:
                        chunk(g, CHUNK_AT.index(n))

            group(0, 0)
            group(1, 2 * KT)
            with dve.Fori(2, GROUPS) as g:
                group(g, 4 * KT, g - 2, 2 * KT)
            columns_of(GROUPS, 0)
            for c in range(4):
                chunk(GROUPS, c)
            hi_n[0] += KT
            sq_n[0] = 2
            t_n[0] = KT
            for j in range(4):
                lo(qc_lo[:, j, :], ps[:, j, :], qc_hi[:, j, :], C_SCALE).then_inc(free[j], 1)

            def nmax(j, keys):
                for qt in range(2):
                    n = 2 * j + qt
                    dve.wait_ge(scores_done, n + 1)
                    if n >= 2:
                        dve.wait_ge(exp_done, n - 1)
                    dve.tensor_reduce(small[:, 40 + qt:41 + qt], ps[:, 4 + qt, 0:keys], AX.X, ALU.max, negate=True)\
                        .then_inc(nmax_ready, 1)

            def normalise(j, keys):
                for qt in range(2):
                    dve.wait_ge(exp_done, 2 * j + qt + 1)
                    link(dve.reciprocal(small[:, 44 + qt:45 + qt], small[:, 42 + qt:43 + qt]))
                    dve.tensor_scalar(prob[:, qt, 0:keys], prob[:, qt, 0:keys], small[:, 44 + qt:45 + qt], None,
                                      ALU.mult).then_inc(prob_ready, 1)

            def turned_lo(keys, pt_hi, pt_lo):
                nk = keys // P
                for qt in range(2):
                    q = slice(qt * P, (qt + 1) * P)
                    lo(pt_lo[:, 0:nk, q], ps[:, 6 + qt, 0:keys].rearrange("p (k q) -> p k q", k=nk),
                       pt_hi[:, 0:nk, q]).then_inc(free[6 + qt], 1)

            def mix(j, r, tile, q0):
                dve.wait_ge(av_done, j + 1)
                dve.tensor_tensor(z[:, tile, q0:q0 + SEQ], ps[:, 2 + r % 2, 0:SEQ], z[:, tile, q0:q0 + SEQ], ALU.mult)\
                    .then_inc(free[2 + r % 2], 1)

            for l in range(DEPTH):
                nt = query_tiles(l)
                nq = nt * P
                if l:
                    link(dve.scalar_tensor_tensor(out=a_col[:, :, :], in0=mods[:, :, 48 * l + KT:48 * l + 2 * KT], scalar=1.0,
                                                  in1=cols[:, Q_NG + KT * l:Q_NG + KT * (l + 1)].unsqueeze(1)
                                                  .broadcast_to([P, 2, KT]), op0=ALU.add, op1=ALU.mult))
                    p = PLAN["head", l]
                    dve.wait_ge(job_done, p["job"] + 1)
                    mean_square(4, D, 4)
                    rsqrt(4)
                    for c in range(4):
                        ins = dve.tensor_scalar(tmp[:, 3, c * P:(c + 1) * P], ident, small[:, 10 + c:11 + c], None, ALU.mult)
                    ins.then_inc(op_ready, 1)
                    dve.wait_ge(job_done, p["job"] + 2)
                    u = PLAN["v_c", l]["unit"]

                    def scaled(k):
                        if k >= 2:
                            dve.wait_ge(op_ready, p["ready"] + k)
                        for v in range(2):
                            t = slice(v * SEQ, (v + 1) * SEQ)
                            ins = dve.scalar_tensor_tensor(out=tmp[:, k % 2, t], in0=z[:, k, t], scalar=a_col[:, v, k:k + 1],
                                                           in1=ps[:, 5, t], op0=ALU.mult, op1=ALU.mult)
                        ins.then_inc(t_ready, 1)

                    scaled(0)
                    t0 = t_n[0]
                    for k in range(KT):
                        if 0 < k < KT - 1:
                            scaled(k + 1)
                        next_hi()
                        dve.wait_ge(t_ready, t0 + k + 1)
                        for v in range(2):
                            t = slice(v * SEQ, (v + 1) * SEQ)
                            ins = dve.scalar_tensor_tensor(out=h_lo[:, k, t], in0=tmp[:, k % 2, t],
                                                           scalar=mods[:, v, 48 * l + k:48 * l + k + 1],
                                                           in1=h_hi[:, k, t].bitcast(F32), op0=ALU.add, op1=ALU.subtract)
                        ins.then_inc(op_ready, 1)
                        if k == 0:
                            scaled(1)
                        if k >= 2:
                            prep_ahead(u + k - 2)
                    t_n[0] += KT
                    prep_ahead(u + KT - 2)
                    prep_ahead(u + KT - 1)
                else:
                    block = ada_block(l, "v_c")
                    for k in range(KT):
                        prep_ahead(PLAN["v_c", l]["unit"] + k)
                        ada_add(block, k)
                for tt in range(4):
                    b = V_C_BANK[l] + tt
                    lo(vc_lo[:, tt, :], ps[:, b, :], vc_hi[:, tt, :]).then_inc(free[b], 1)
                ada(l, "v_c")

                def split_tile(dst_lo, dst_hi, n, scale, h0):
                    def evac(i, j):
                        dve.wait_ge(op_hi, h0 + 1 + j + 2 * i)
                        t = bass.ds(2 * i + j, 1)
                        dve.scalar_tensor_tensor(out=dst_lo[:, t, 0:n], in0=ps[:, j:j + 1, 0:n], scalar=scale,
                                                 in1=dst_hi[:, t, 0:n].bitcast(F32), op0=ALU.mult, op1=ALU.subtract)\
                            .then_inc(free[j], 1)
                    return evac

                if l:
                    tiles("q_c", l, split_tile(qc_lo, qc_hi, nq, C_SCALE, hi_n[0]))
                    hi_n[0] += 4
                tiles("k_c", l, split_tile(kc_lo, kc_hi, TOK, 1.0, hi_n[0]))
                hi_n[0] += 4
                ada(l, "k_c")
                tiles("g_c", l, None)

                def attention(name, heads, tile0, pt_hi, pt_lo, operands):
                    jobs = att_jobs(l, heads)
                    p = PLAN[name, l]
                    for r in range(-1, len(jobs) + 1):
                        if r + 1 < len(jobs):
                            h, q0, k0 = jobs[r + 1]
                            if operands and q0 == 0 and h + 1 < heads:
                                operands(h + 1)
                            j = p["att"] + r + 1
                            nmax(j, TOK - k0)
                            normalise(j, TOK - k0)
                        if 0 <= r < len(jobs):
                            turned_lo(TOK - jobs[r][2], pt_hi, pt_lo)
                            for m in early_tiles(l, r) if operands else ():
                                lo(oa_lo[:, m, 0:nq], z[:, OUT_TILES[m], 0:nq], oa_hi[:, m, 0:nq]).then_inc(op_ready, 1)
                        if r >= 1:
                            h, q0, k0 = jobs[r - 1]
                            mix(p["att"] + r - 1, r - 1, tile0 + h, q0)

                dve.wait_ge(free[1], PLAN["att_c", l][1])
                dve.wait_ge(free[0], PLAN["att_c", l][0])
                attention("att_c", HEADS_C, 12, ptc_hi, ptc_lo, None)

                ada(l, "g_c")
                p = PLAN["v_a", l]
                block = ada_block(l, "v_a")
                for k in range(KT):
                    prep_ahead(p["unit"] + k)
                    ada_add(block, k)

                def gate_norm(n):
                    p = PLAN["v_a", l]
                    if n < nt:
                        dve.wait_ge(free[n], p[n] + 1)
                        link(dve.tensor_tensor_reduce(tmp[:, 0, :], z[:, VA + n, :], z[:, VA + n, :], 1.0, 0.0,
                                                      ALU.mult, ALU.add, small[:, 30 + n:31 + n]))
                    elif n == nt:
                        link(dve.tensor_scalar(small[:, 0:nt], small[:, 30:30 + nt], 1.0 / W_A, EPS, ALU.mult, ALU.add))
                        rsqrt(nt)
                    elif n <= 2 * nt:
                        tt = n - nt - 1
                        if tt == 0:
                            dve.wait_ge(gate_in, 48 * (l + 1))
                        ins = dve.scalar_tensor_tensor(out=z[:, VA + tt, :], in0=z[:, VA + tt, :],
                                                       scalar=small[:, 10 + tt:11 + tt], in1=sgu_row[:, :],
                                                       op0=ALU.mult, op1=ALU.mult)
                        if tt == nt - 1:
                            ins.then_inc(op_ready, 1)
                    elif n == 2 * nt + 1:
                        dve.wait_ge(job_done, PLAN["w_s", l]["job"] + 1)
                        dve.tensor_copy(ws_t[:, :, :].rearrange("p g q -> p (g q)"), ps[:, 4, :]).then_inc(op_ready, 1)

                ada(l, "v_a")
                tiles("u", l, None, between=gate_norm)
                ada(l, "u")
                tiles("g_a", l, None)
                ada(l, "g_a")

                def gate_mix(m):
                    if m >= 4:
                        return
                    p, g = PLAN["mix_a", l], m
                    if g == 0:
                        dve.wait_ge(op_ready, p["ready"])
                        dve.wait_ge(free[0], p[0])
                        dve.wait_ge(free[1], p[1])
                    link(dve.tensor_tensor(z[:, g, 0:nq], z[:, g, 0:nq], z[:, UG + g, 0:nq], ALU.mult))
                    dve.wait_ge(job_done, p["job"] + g + 1)
                    dve.tensor_tensor(tmp[:, g % 2, 0:nq].rearrange("p (t q) -> p t q", t=nt),
                                      ps[:, 2 + g, 0:nq].rearrange("p (t q) -> p t q", t=nt),
                                      bs_row[:, g, :].unsqueeze(1).broadcast_to([P, nt, P]), ALU.add)\
                        .then_inc(free[2 + g], 1)
                    dve.wait_ge(free[2 + g], p[2 + g] + 1)
                    ins = dve.tensor_tensor(z[:, g, 0:nq], z[:, g, 0:nq], tmp[:, g % 2, 0:nq], ALU.mult)
                    if g < 3:
                        link(ins)
                    else:
                        ins.then_inc(op_ready, 1)
                        for a in range(2):
                            link(dve.memset(tmp[:, 2 + a, :], 0.0))

                def latent_square(acc, n):
                    sq0 = sq_n[0]
                    def evac(i, j):
                        dve.wait_ge(sq_ready, sq0 + 1 + j + 2 * i)
                        dve.wait_ge(sq_sum, sq0 + j + 2 * i)
                        dve.tensor_tensor(tmp[:, acc, 0:n], tmp[:, acc, 0:n], tmp[:, j, 0:n], ALU.add)\
                            .then_inc(sq_sum, 1)
                    return evac

                tiles("cq", l, latent_square(2, nq), between=gate_mix)
                sq_n[0] += 4
                ada(l, "cq")
                tiles("ckv", l, latent_square(3, TOK))
                sq_n[0] += 4
                ada(l, "ckv")

                p = PLAN["lat", l]
                dve.wait_ge(job_done, p["job"] + 1)
                mean_square(nt + 4, LORA, 4)
                rsqrt(nt + 4)
                for a, (c0, n) in enumerate(((0, nt), (nt, 4))):
                    for c in range(n):
                        ins = dve.tensor_scalar(tmp[:, a, c * P:(c + 1) * P], ident, small[:, 10 + c0 + c:11 + c0 + c],
                                                None, ALU.mult)
                    ins.then_inc(op_ready, 1)
                for q in range(4):
                    prep_ahead(PLAN["kr", l]["unit"] + q)

                u = PLAN["g_b", l]["unit"]

                def latent_normed(s):
                    n = nq if s < KL else TOK
                    if s in (0, KL):
                        dve.wait_ge(job_done, p["job"] + (2 if s == 0 else 3))
                    if s >= 2:
                        dve.wait_ge(op_ready, PLAN["latn", l]["ready"] + s - 1)
                    g = (Q_QA if s < KL else Q_KV) + KL * l + s % KL
                    dve.scalar_tensor_tensor(out=tmp[:, 2 + s % 2, 0:n], in0=z[:, RAWL + s, 0:n],
                                             scalar=cols[:, g:g + 1],
                                             in1=ps[:, 5 if s < KL else 4, 0:n], op0=ALU.mult, op1=ALU.mult)\
                        .then_inc(t_ready, 1)

                latent_normed(0)
                t0 = t_n[0]
                for m in range(16):
                    if m % 2 == 0:
                        s = m // 2
                        if s + 1 < 8:
                            latent_normed(s + 1)
                        n = nq if s < KL else TOK
                        dh, dl = (cq_hi, cq_lo) if s < KL else (cv_hi, cv_lo)
                        dve.wait_ge(t_ready, t0 + s + 1)
                        lo(dl[:, s % KL, 0:n], tmp[:, 2 + s % 2, 0:n], dh[:, s % KL, 0:n]).then_inc(op_ready, 1)
                    prep_ahead(u + m)
                t_n[0] += 8
                k = PLAN["kr", l]
                dve.wait_ge(job_done, k["job"] + 1)
                dve.tensor_tensor(prob[:, 1, 0:SEQ], prob[:, 0, 0:SEQ], cos, ALU.mult)
                dve.tensor_tensor(prob[:, 1, SEQ:TOK], ps[:, 3, 0:SEQ], sin, ALU.mult).then_inc(free[3], 1)
                dve.wait_ge(free[3], k[3] + 1)
                dve.tensor_tensor(prob[:, 0, 0:SEQ], prob[:, 1, 0:SEQ], prob[:, 1, SEQ:TOK], ALU.add).then_inc(t_ready, 1)
                t_n[0] += 1
                dve.wait_ge(t_ready, t_n[0])
                lo(kr_ab[0:ROPE, 1, :], prob[0:ROPE, 0, :], kr_ab[0:ROPE, 0, :]).then_inc(op_ready, 1)
                lo(kr_ab[ROPE:P, 3, :], prob[ROPE:P, 0, :], kr_ab[ROPE:P, 2, :]).then_inc(op_ready, 1)
                tiles("g_b", l, None, 8, 2)

                u = PLAN["v_b", l]["unit"]
                for half in range(2):
                    for k in range(KL):
                        prep_ahead(u + 4 * half + k)
                    if half == 0:
                        ada(l, "g_b")
                    for tt in range(4):
                        c = slice(half * 512, half * 512 + 512)
                        b = 4 * half + tt
                        lo(v_lo[:, tt, c], ps[:, b, :], v_hi[:, tt, c]).then_inc(free[b], 1)

                p = PLAN["q_r", l]
                for pair in range(5):
                    if pair < 4:
                        prep_ahead(p["unit"] + pair)
                    if pair >= 1:
                        m = pair - 1
                        dve.wait_ge(job_done, p["job"] + m + 1)
                        dst = tmp[:, 2 + m % 2, :]
                        dve.scalar_tensor_tensor(out=tmp[:, 0, 0:SEQ], in0=prob[:, m % 2, 0:SEQ], scalar=MLA_SCALE,
                                                 in1=cos, op0=ALU.mult, op1=ALU.mult)
                        dve.scalar_tensor_tensor(out=tmp[:, 1, 0:SEQ], in0=ps[:, 2 + m % 2, 0:SEQ], scalar=MLA_SCALE,
                                                 in1=sin, op0=ALU.mult, op1=ALU.mult).then_inc(free[2 + m % 2], 1)
                        dve.wait_ge(free[2 + m % 2], p[2 + m % 2] + m // 2 + 1)
                        if nq > SEQ:
                            dve.tensor_scalar(dst[:, SEQ:TOK], prob[:, m % 2, SEQ:TOK], MLA_SCALE, None, ALU.mult)
                        dve.tensor_tensor(dst[:, 0:SEQ], tmp[:, 0, 0:SEQ], tmp[:, 1, 0:SEQ], ALU.add).then_inc(t_ready, 1)
                        t_n[0] += 1
                        dve.wait_ge(t_ready, t_n[0])
                        lo(qr_lo[:, m, 0:nq], dst[:, 0:nq], qr_hi[:, m, 0:nq]).then_inc(op_ready, 1)

                p = PLAN["heads", l]

                def head_operands(h):
                    prep_ahead(p["unit"] + 2 * h)
                    lo(qk_lo[:, h % 2, 0:nq], ps[:, 0, 0:nq], qk_hi[:, h % 2, 0:nq], MLA_SCALE).then_inc(free[0], 1)
                    prep_ahead(p["unit"] + 2 * h + 1)
                    lo(qk_lo[:, 2 + h % 2, :], ps[:, 1, :], qk_hi[:, 2 + h % 2, :]).then_inc(free[1], 1)

                head_operands(0)
                attention("heads", HEADS_B, 4, ptb_hi, ptb_lo, head_operands)

                p = PLAN["out", l]
                u = p["unit"]
                link(dve.memset(tmp[:, 2, :], 0.0))
                gate = 48 * l + 2 * KT

                def new_x(i, j):
                    dve.wait_ge(unit_done, u + (6 if isinstance(i, int) and i == j == 0 else 4 * (j + 1)) + 8 * i)
                    dve.wait_ge(x_back[j], 16 * (KT // 2) * l + 16 * (i + 1))
                    t = bass.ds(2 * i + j, 1)
                    for v in range(nq // SEQ):
                        c = slice(v * SEQ, (v + 1) * SEQ)
                        ins = dve.scalar_tensor_tensor(out=z[:, t, c], in0=ps[:, j:j + 1, c],
                                                       scalar=mods[:, v, bass.ds(gate + 2 * i + j, 1)],
                                                       in1=x_res[:, j:j + 1, c], op0=ALU.mult, op1=ALU.add)
                    ins.then_inc(free[j], 1)

                sq0 = sq_n[0]

                def square(i, j):
                    dve.wait_ge(sq_ready, sq0 + 1 + j + 2 * i)
                    dve.wait_ge(sq_sum, sq0 + j + 2 * i)
                    dve.tensor_tensor(tmp[:, 2, 0:nq], tmp[:, 2, 0:nq], tmp[:, j, 0:nq], ALU.add).then_inc(sq_sum, 1)

                for n in range(2):
                    prep_ahead(u + n)
                for m in range(8):
                    lo(ob_lo[:, m, 0:nq], z[:, OUT_TILES[8 + m], 0:nq], ob_hi[:, m, 0:nq]).then_inc(op_ready, 1)
                    if m % 4 == 3:
                        prep_ahead(u + 2 + m // 4)
                for s in range(4, 8):
                    prep_ahead(u + s)
                new_x(0, 0)
                square(0, 0)
                new_x(0, 1)

                def turn_pair(i, u8, per, block=None, start=0):
                    for s in range(8):
                        if s == 4:
                            square(i - 1, 1)
                            new_x(i, 0)
                        prep_ahead(u8 + s, i if per else 0, per)
                        ada_add(block, s, i - start)
                    square(i, 0)
                    new_x(i, 1)

                if l == 0:
                    for first in (1, 3, 5):
                        block = ada_block(l, f"out{first}")
                        with dve.Fori(first, first + 2) as i:
                            turn_pair(i, u, 8, block, first)
                        ada(l, f"out{first}")
                    turn_pair(KT // 2 - 1, u + 8 * (KT // 2 - 1), 0)
                else:
                    with dve.Fori(1, KT // 2 - 1) as i:
                        turn_pair(i, u, 8)
                    turn_pair(KT // 2 - 1, u + 8 * (KT // 2 - 1), 0)
                square(KT // 2 - 1, 1)
                sq_n[0] += KT

            p = PLAN["end", 0]
            dve.wait_ge(job_done, p["job"] + 5)
            mean_square(2, D, 4)
            rsqrt(2, final_rms)
            for n in range(0, 8, 2):
                tt, g, b = n // 4, n % 4, FINAL_BANKS[n]
                dve.wait_ge(job_done, p["job"] + (n + 1 if n < 4 else n + 2))
                dve.tensor_scalar(y[:, tt, g * 512:(g + 1) * 512], ps[:, b, :], small[:, 10 + tt:11 + tt], None,
                                  ALU.mult).then_inc(free[b], 1)


def constants():
    f = np.float32
    c = np.zeros((P, C_N), f)
    c[:, C_ID:C_ID + P] = np.eye(P, dtype=f)
    q = ROPE // 4
    for m in range(P):
        b = m % (2 * q)
        if b < q:
            c[m + q, C_ROT + m] = -1.0
        else:
            c[m - q, C_ROT + m] = 1.0
    t = np.arange(SEQ)
    inv = f(10000.0) ** (-np.arange(q, dtype=f) / f(q))
    pos = np.stack([(t // GRID_W).astype(f), (t % GRID_W).astype(f)])
    for m in range(P):
        ang = (pos[(m % ROPE) // (2 * q)] * inv[m % q]).astype(f)
        c[m, C_COS:C_COS + SEQ] = np.cos(ang)
        c[m, C_SIN:C_SIN + SEQ] = np.sin(ang)
    col = np.arange(GRID_W)
    c0 = np.clip(col - 8, 0, GRID_W - 16)
    ok = (col[None, :] >= c0[:, None]) & (col[None, :] < c0[:, None] + 16)
    ok = np.concatenate([ok, ok])
    ok = ok[::-1]
    c[:, C_TURN:C_TURN + P] = np.kron(np.eye(2), np.eye(GRID_W)[::-1]).astype(f)
    c[:, C_KEEP:C_KEEP + GRID_W] = ok
    c[:, C_MASK:C_MASK + GRID_W] = np.where(ok, f(0), f(NEG))
    return c


def kernel(**inputs):
    import concourse.bacc as bacc
    from concourse.bass_utils import run_bass_kernel_spmd

    a = {n: np.ascontiguousarray(v) for n, v in inputs.items()}
    rows = {
        "rows_a": np.concatenate([a["c"].reshape(KT, P), a["c_ctx"].reshape(KT, P), a["norm_g"].reshape(-1, P),
                                  a["qa_g"].reshape(-1, P), a["kva_g"].reshape(-1, P), a["final_g"].reshape(-1, P)]),
        "rows_b": a["b_ada"].reshape(-1, P),
        "consts": constants(),
    }
    nc = bacc.Bacc("TRN2", target_bir_lowering=False, num_devices=1)
    arrays, args = {}, []
    names = ["x", "ctx", "w_ada", "w_in", "w_uq", "w_ukv", "sgu_g", "w_s", "b_s", "rpb", "w_out"]
    for n in names + list(rows):
        v = np.ascontiguousarray(a[n] if n in names else rows[n])
        arrays[f"in_{n}"] = v
        args.append(nc.dram_tensor(f"in_{n}", v.shape, mybir.dt.from_np(v.dtype), kind="ExternalInput").ap())
    args.append(nc.dram_tensor("out_x", (1, SEQ, D), F32, kind="ExternalOutput").ap())
    hybrid_kernel(nc, *args)
    r = run_bass_kernel_spmd(nc, [arrays], core_ids=[0])
    return r.results[0]["out_x"]
```
